# Optimizing a Trainium2 kernel written in Bass

```python
import math
import jax
import jax.numpy as jnp
from jax import lax
import numpy as np
import jax, jax.numpy as jnp

D_MODEL = 1024
BATCH = 1
SEQ = 512
DEPTH = 2

CHUNK = 64
Q_BLOCK = 128
ROPE_THETA = 10000.0
NORM_EPS = 1e-6
F32 = jnp.float32

SSM_HEAD_DIM = 64
SSM_HEADS = D_MODEL // SSM_HEAD_DIM
SSM_INNER = SSM_HEADS * SSM_HEAD_DIM
SSM_STATE = 128
SSM_GROUPS = 2
CONV_WIDTH = 4
SSM_CONV_CH = SSM_INNER + 2 * SSM_GROUPS * SSM_STATE

DIFF_HEAD_DIM = 64
DIFF_HEADS = D_MODEL // (2 * DIFF_HEAD_DIM)
DIFF_WIDTH = DIFF_HEADS * 2 * DIFF_HEAD_DIM

EVEN_SIZES = (SSM_INNER, SSM_CONV_CH, SSM_HEADS, DIFF_WIDTH, DIFF_WIDTH, DIFF_WIDTH)
EVEN_IN = SSM_INNER + SSM_CONV_CH + SSM_HEADS + 3 * DIFF_WIDTH
EVEN_MIX = SSM_INNER + DIFF_WIDTH

S5_WIDTH = D_MODEL // 2
S5_GROUP = 16
S5_GROUPS = S5_WIDTH // S5_GROUP
S5_STATE = 64

MLA_HEADS = 8
MLA_NOPE = 64
MLA_ROPE = 32
MLA_V = 64
MLA_Q_RANK = 384
MLA_KV_RANK = 256
MLA_WIDTH = MLA_HEADS * MLA_V

ODD_SIZES = (S5_WIDTH, MLA_Q_RANK, MLA_KV_RANK, MLA_ROPE)
ODD_IN = S5_WIDTH + MLA_Q_RANK + MLA_KV_RANK + MLA_ROPE
ODD_MIX = S5_WIDTH + MLA_WIDTH

FFN_HIDDEN = ((8 * D_MODEL + 3 * 256 - 1) // (3 * 256)) * 256
N_EVEN = (DEPTH + 1) // 2
N_ODD = DEPTH // 2


def rms_norm(x, g):
    xf = x.astype(F32)
    y = xf * lax.rsqrt(jnp.mean(xf * xf, axis=-1, keepdims=True) + NORM_EPS)
    return (y * g.astype(F32)).astype(x.dtype)

def split_cols(x, sizes):
    cuts, acc = [], 0
    for s in sizes[:-1]:
        acc += s
        cuts.append(acc)
    return jnp.split(x, cuts, axis=-1)

def rope(x, pos):
    d = x.shape[-1]
    half = d // 2
    inv_freq = ROPE_THETA ** (-jnp.arange(half, dtype=F32) * (2.0 / d))
    ang = pos.astype(F32)[:, :, None] * inv_freq
    cos = jnp.cos(ang)[:, :, None, :]
    sin = jnp.sin(ang)[:, :, None, :]
    xf = x.astype(F32)
    x1, x2 = xf[..., :half], xf[..., half:]
    return jnp.concatenate([x1 * cos - x2 * sin, x2 * cos + x1 * sin], axis=-1).astype(x.dtype)

def chunk_causal_mask(start, seq_len):
    qi = start + jnp.arange(Q_BLOCK, dtype=jnp.int32)
    kj = jnp.arange(seq_len, dtype=jnp.int32)
    return (kj[None, :] // CHUNK) <= (qi[:, None] // CHUNK)

def masked_softmax(s, mask):
    return jax.nn.softmax(jnp.where(mask, s.astype(F32), -jnp.inf), axis=-1)

def sweep_query_blocks(fn, *qs):
    bsz, s = qs[0].shape[:2]
    nb = s // Q_BLOCK
    blocks = tuple(jnp.swapaxes(q.reshape(bsz, nb, Q_BLOCK, *q.shape[2:]), 0, 1) for q in qs)
    starts = jnp.arange(nb, dtype=jnp.int32) * Q_BLOCK
    out = lax.map(lambda a: fn(*a), (starts, *blocks))
    out = jnp.swapaxes(out, 0, 1)
    return out.reshape(bsz, s, *out.shape[3:])

def causal_depthwise_conv(x, w, b):
    k, ch = w.shape
    y = lax.conv_general_dilated(x, w[:, None, :].astype(x.dtype), window_strides=(1,),
                                 padding=[(k - 1, 0)], dimension_numbers=('NWC', 'WIO', 'NWC'),
                                 feature_group_count=ch)
    return y + b.astype(x.dtype)

def ssd_chunked_scan(x, dt, a, b, c):
    bsz, s, h, p = x.shape
    g, n = b.shape[2], b.shape[3]
    r = h // g
    nc = s // CHUNK
    x = x.reshape(bsz, nc, CHUNK, g, r, p)
    dt = dt.reshape(bsz, nc, CHUNK, g, r)
    b = b.reshape(bsz, nc, CHUNK, g, n)
    c = c.reshape(bsz, nc, CHUNK, g, n)
    xdt = x * dt[..., None]
    a_cs = jnp.cumsum(dt * a.reshape(g, r), axis=2)
    seg = a_cs[:, :, :, None] - a_cs[:, :, None, :]
    causal = jnp.tril(jnp.ones((CHUNK, CHUNK), dtype=bool))[:, :, None, None]
    decay = jnp.exp(jnp.where(causal, seg, -jnp.inf))
    cb = jnp.einsum('bclgn,bcsgn->bclsg', c, b)
    y_diag = jnp.einsum('bclsgr,bcsgrp->bclgrp', cb[..., None] * decay, xdt)
    decay_states = jnp.exp(a_cs[:, :, -1:] - a_cs)
    states = jnp.einsum('bclgn,bclgrp->bcgrpn', b, decay_states[..., None] * xdt)
    chunk_decay = jnp.exp(a_cs[:, :, -1])

    def step(hs, inp):
        s_c, d_c = inp
        return hs * d_c[..., None, None] + s_c, hs

    _, prev = lax.scan(step, jnp.zeros_like(states[:, 0]),
                       (jnp.moveaxis(states, 1, 0), jnp.moveaxis(chunk_decay, 1, 0)))
    prev = jnp.moveaxis(prev, 0, 1)
    y_off = jnp.einsum('bclgn,bcgrpn->bclgrp', c, prev) * jnp.exp(a_cs)[..., None]
    return (y_diag + y_off).reshape(bsz, s, h, p)

def mamba2_group(z, xbc, dt_raw, conv_w, conv_b, dt_bias, a_log, d_skip, gate_norm):
    bsz, s, _ = z.shape
    xbc = jax.nn.silu(causal_depthwise_conv(xbc, conv_w, conv_b))
    xs, bs, cs = split_cols(xbc, (SSM_INNER, SSM_GROUPS * SSM_STATE, SSM_GROUPS * SSM_STATE))
    xs = xs.reshape(bsz, s, SSM_HEADS, SSM_HEAD_DIM).astype(F32)
    dt = jax.nn.softplus(dt_raw.astype(F32) + dt_bias.astype(F32))
    a = -jnp.exp(a_log.astype(F32))
    y = ssd_chunked_scan(xs, dt, a,
                         bs.reshape(bsz, s, SSM_GROUPS, SSM_STATE).astype(F32),
                         cs.reshape(bsz, s, SSM_GROUPS, SSM_STATE).astype(F32))
    y = y + d_skip.astype(F32)[:, None] * xs
    y = y.reshape(bsz, s, SSM_INNER) * jax.nn.silu(z.astype(F32))
    return rms_norm(y, gate_norm).astype(z.dtype)

def diff_attention_group(q, k, v, pos, layer, lambdas, subln):
    bsz, s, _ = q.shape
    hh, d = DIFF_HEADS, DIFF_HEAD_DIM
    q = rope(q.reshape(bsz, s, 2 * hh, d), pos).reshape(bsz, s, hh, 2, d)
    k = rope(k.reshape(bsz, s, 2 * hh, d), pos).reshape(bsz, s, hh, 2, d)
    vf = v.reshape(bsz, s, hh, 2 * d).astype(F32)
    k1, k2 = k[:, :, :, 0], k[:, :, :, 1]
    lam_init = 0.8 - 0.6 * math.exp(-0.3 * layer)
    lf = lambdas.astype(F32)
    lam = jnp.exp(jnp.sum(lf[0] * lf[1])) - jnp.exp(jnp.sum(lf[2] * lf[3])) + lam_init
    scale = d ** -0.5

    def block(start, q1b, q2b):
        mask = chunk_causal_mask(start, s)
        p1 = masked_softmax(jnp.einsum('bqhd,bkhd->bhqk', q1b, k1, preferred_element_type=F32) * scale, mask)
        p2 = masked_softmax(jnp.einsum('bqhd,bkhd->bhqk', q2b, k2, preferred_element_type=F32) * scale, mask)
        return jnp.einsum('bhqk,bkhe->bqhe', p1 - lam * p2, vf)

    o = sweep_query_blocks(block, q[:, :, :, 0], q[:, :, :, 1])
    o = rms_norm(o, subln) * (1.0 - lam_init)
    return o.reshape(bsz, s, DIFF_WIDTH).astype(q.dtype)

def s5_combine(e1, e2):
    a1, b1 = e1
    a2, b2 = e2
    return a1 * a2, a2 * b1 + b2

def s5_group(u, lam_re, lam_im, log_step, b_re, b_im, c_re, c_im, d_skip, w_glu, b_glu):
    bsz, s, _ = u.shape
    ug = u.reshape(bsz, s, S5_GROUPS, S5_GROUP).astype(F32)
    lam = lax.complex(lam_re.astype(F32), lam_im.astype(F32))
    delta = jnp.exp(log_step.astype(F32))[:, None]
    a_bar = jnp.exp(lam * delta)
    b_bar = ((a_bar - 1.0) / lam)[..., None] * lax.complex(b_re.astype(F32), b_im.astype(F32))
    bu = jnp.einsum('bsgh,gph->bsgp', ug.astype(jnp.complex64), b_bar)
    a_el = jnp.broadcast_to(a_bar, bu.shape)
    _, state = lax.associative_scan(s5_combine, (a_el, bu), axis=1)
    cm = lax.complex(c_re.astype(F32), c_im.astype(F32))
    y = jnp.real(jnp.einsum('bsgp,ghp->bsgh', state, cm)) + d_skip.astype(F32).reshape(S5_GROUPS, S5_GROUP) * ug
    y = jax.nn.gelu(y.reshape(bsz, s, S5_WIDTH))
    y = y * jax.nn.sigmoid(y @ w_glu.astype(F32) + b_glu.astype(F32))
    return y.astype(u.dtype)

def mla_group(c_q, c_kv, k_rope, pos, q_norm, w_uq, kv_norm, w_ukv):
    bsz, s, _ = c_q.shape
    q = (rms_norm(c_q, q_norm) @ w_uq).reshape(bsz, s, MLA_HEADS, MLA_NOPE + MLA_ROPE)
    q_nope, q_rot = q[..., :MLA_NOPE], rope(q[..., MLA_NOPE:], pos)
    kv = (rms_norm(c_kv, kv_norm) @ w_ukv).reshape(bsz, s, MLA_HEADS, MLA_NOPE + MLA_V)
    k_nope, vf = kv[..., :MLA_NOPE], kv[..., MLA_NOPE:].astype(F32)
    k_rot = rope(k_rope[:, :, None, :], pos)[:, :, 0, :]
    scale = (MLA_NOPE + MLA_ROPE) ** -0.5

    def block(start, qn, qr):
        sc = (jnp.einsum('bqhd,bkhd->bhqk', qn, k_nope, preferred_element_type=F32)
              + jnp.einsum('bqhr,bkr->bhqk', qr, k_rot, preferred_element_type=F32))
        p = masked_softmax(sc * scale, chunk_causal_mask(start, s))
        return jnp.einsum('bhqk,bkhe->bqhe', p, vf)

    o = sweep_query_blocks(block, q_nope, q_rot)
    return o.reshape(bsz, s, MLA_WIDTH).astype(c_q.dtype)

def even_mixer(h, pos, layer, w_in, conv_w, conv_b, dt_bias, a_log, d_skip, gate_norm, lambdas, subln, w_out):
    z, xbc, dt_raw, q, k, v = split_cols(h @ w_in, EVEN_SIZES)
    y_a = mamba2_group(z, xbc, dt_raw, conv_w, conv_b, dt_bias, a_log, d_skip, gate_norm)
    y_b = diff_attention_group(q, k, v, pos, layer, lambdas, subln)
    return jnp.concatenate([y_a, y_b], axis=-1) @ w_out

def odd_mixer(h, pos, w_in, lam_re, lam_im, log_step, b_re, b_im, c_re, c_im, d_skip, w_glu, b_glu,
              q_norm, w_uq, kv_norm, w_ukv, w_out):
    u, c_q, c_kv, k_rope = split_cols(h @ w_in, ODD_SIZES)
    y_c = s5_group(u, lam_re, lam_im, log_step, b_re, b_im, c_re, c_im, d_skip, w_glu, b_glu)
    y_d = mla_group(c_q, c_kv, k_rope, pos, q_norm, w_uq, kv_norm, w_ukv)
    return jnp.concatenate([y_c, y_d], axis=-1) @ w_out

def swiglu(x, wg, wu, wd):
    return (jax.nn.silu(x @ wg) * (x @ wu)) @ wd

def first_inputs(seed: int = 0) -> dict:
    key = jax.random.key(seed)
    ks = iter(jax.random.split(key, 48))

    def nrm(shape, scale):
        return jax.random.normal(next(ks), shape, F32) * scale

    def gain(shape):
        return 1.0 + nrm(shape, 0.01)

    def log_uniform(shape, lo, hi):
        return jax.random.uniform(next(ks), shape, F32, minval=math.log(lo), maxval=math.log(hi))

    x = nrm((BATCH, SEQ, D_MODEL), 1.0)
    start = jax.random.randint(next(ks), (BATCH,), 0, 1024, dtype=jnp.int32) * CHUNK
    positions = start[:, None] + jnp.arange(SEQ, dtype=jnp.int32)[None, :]
    norm_mix = gain((DEPTH, D_MODEL))
    ev_w_in = nrm((N_EVEN, D_MODEL, EVEN_IN), D_MODEL ** -0.5)
    ev_conv_w = nrm((N_EVEN, CONV_WIDTH, SSM_CONV_CH), CONV_WIDTH ** -0.5)
    ev_conv_b = nrm((N_EVEN, SSM_CONV_CH), 0.01)
    dt0 = jnp.exp(log_uniform((N_EVEN, SSM_HEADS), 1e-3, 1e-1))
    ev_dt_bias = dt0 + jnp.log(-jnp.expm1(-dt0))
    ev_a_log = jnp.log(jax.random.uniform(next(ks), (N_EVEN, SSM_HEADS), F32, minval=1.0, maxval=16.0))
    ev_d_skip = gain((N_EVEN, SSM_HEADS))
    ev_gate_norm = gain((N_EVEN, SSM_INNER))
    ev_lambdas = nrm((N_EVEN, 4, DIFF_HEAD_DIM), 0.1)
    ev_subln = gain((N_EVEN, 2 * DIFF_HEAD_DIM))
    ev_w_out = nrm((N_EVEN, EVEN_MIX, D_MODEL), EVEN_MIX ** -0.5)
    od_w_in = nrm((N_ODD, D_MODEL, ODD_IN), D_MODEL ** -0.5)
    od_lam_re = -0.5 + nrm((N_ODD, S5_GROUPS, S5_STATE), 0.01)
    od_lam_im = math.pi * jnp.arange(S5_STATE, dtype=F32) + nrm((N_ODD, S5_GROUPS, S5_STATE), 0.01)
    od_log_step = log_uniform((N_ODD, S5_GROUPS), 1e-3, 1e-1)
    od_b_re = nrm((N_ODD, S5_GROUPS, S5_STATE, S5_GROUP), (2 * S5_GROUP) ** -0.5)
    od_b_im = nrm((N_ODD, S5_GROUPS, S5_STATE, S5_GROUP), (2 * S5_GROUP) ** -0.5)
    od_c_re = nrm((N_ODD, S5_GROUPS, S5_GROUP, S5_STATE), (2 * S5_STATE) ** -0.5)
    od_c_im = nrm((N_ODD, S5_GROUPS, S5_GROUP, S5_STATE), (2 * S5_STATE) ** -0.5)
    od_d_skip = gain((N_ODD, S5_WIDTH))
    od_w_glu = nrm((N_ODD, S5_WIDTH, S5_WIDTH), S5_WIDTH ** -0.5)
    od_b_glu = nrm((N_ODD, S5_WIDTH), 0.01)
    od_q_norm = gain((N_ODD, MLA_Q_RANK))
    od_w_uq = nrm((N_ODD, MLA_Q_RANK, MLA_HEADS * (MLA_NOPE + MLA_ROPE)), MLA_Q_RANK ** -0.5)
    od_kv_norm = gain((N_ODD, MLA_KV_RANK))
    od_w_ukv = nrm((N_ODD, MLA_KV_RANK, MLA_HEADS * (MLA_NOPE + MLA_V)), MLA_KV_RANK ** -0.5)
    od_w_out = nrm((N_ODD, ODD_MIX, D_MODEL), ODD_MIX ** -0.5)
    norm_ffn = gain((DEPTH, D_MODEL))
    ffn_gate = nrm((DEPTH, D_MODEL, FFN_HIDDEN), D_MODEL ** -0.5)
    ffn_up = nrm((DEPTH, D_MODEL, FFN_HIDDEN), D_MODEL ** -0.5)
    ffn_down = nrm((DEPTH, FFN_HIDDEN, D_MODEL), FFN_HIDDEN ** -0.5)
    norm_final = gain((D_MODEL,))
    return {'x': x, 'positions': positions, 'norm_mix': norm_mix,
            'ev_w_in': ev_w_in, 'ev_conv_w': ev_conv_w, 'ev_conv_b': ev_conv_b,
            'ev_dt_bias': ev_dt_bias, 'ev_a_log': ev_a_log, 'ev_d_skip': ev_d_skip,
            'ev_gate_norm': ev_gate_norm, 'ev_lambdas': ev_lambdas, 'ev_subln': ev_subln,
            'ev_w_out': ev_w_out,
            'od_w_in': od_w_in, 'od_lam_re': od_lam_re, 'od_lam_im': od_lam_im,
            'od_log_step': od_log_step, 'od_b_re': od_b_re, 'od_b_im': od_b_im,
            'od_c_re': od_c_re, 'od_c_im': od_c_im, 'od_d_skip': od_d_skip,
            'od_w_glu': od_w_glu, 'od_b_glu': od_b_glu, 'od_q_norm': od_q_norm,
            'od_w_uq': od_w_uq, 'od_kv_norm': od_kv_norm, 'od_w_ukv': od_w_ukv,
            'od_w_out': od_w_out,
            'norm_ffn': norm_ffn, 'ffn_gate': ffn_gate, 'ffn_up': ffn_up, 'ffn_down': ffn_down,
            'norm_final': norm_final}

def first_block(x, positions, norm_mix,
              ev_w_in, ev_conv_w, ev_conv_b, ev_dt_bias, ev_a_log, ev_d_skip,
              ev_gate_norm, ev_lambdas, ev_subln, ev_w_out,
              od_w_in, od_lam_re, od_lam_im, od_log_step, od_b_re, od_b_im,
              od_c_re, od_c_im, od_d_skip, od_w_glu, od_b_glu, od_q_norm,
              od_w_uq, od_kv_norm, od_w_ukv, od_w_out,
              norm_ffn, ffn_gate, ffn_up, ffn_down, norm_final):
    h = x
    for i in range(DEPTH):
        j = i // 2
        hn = rms_norm(h, norm_mix[i])
        if i % 2 == 0:
            mix = even_mixer(hn, positions, i, ev_w_in[j], ev_conv_w[j], ev_conv_b[j], ev_dt_bias[j],
                             ev_a_log[j], ev_d_skip[j], ev_gate_norm[j], ev_lambdas[j], ev_subln[j],
                             ev_w_out[j])
        else:
            mix = odd_mixer(hn, positions, od_w_in[j], od_lam_re[j], od_lam_im[j], od_log_step[j],
                            od_b_re[j], od_b_im[j], od_c_re[j], od_c_im[j], od_d_skip[j],
                            od_w_glu[j], od_b_glu[j], od_q_norm[j], od_w_uq[j], od_kv_norm[j],
                            od_w_ukv[j], od_w_out[j])
        h = h + mix
        h = h + swiglu(rms_norm(h, norm_ffn[i]), ffn_gate[i], ffn_up[i], ffn_down[i])
    return rms_norm(h, norm_final)


N_MIXERS = 2
ALPHA = (2 * DEPTH) ** 0.25
BETA = (8 * DEPTH) ** -0.25
LN_EPS = 1e-5
N_A = (DEPTH + 1) // 2
N_B = DEPTH // 2
D_FF = 2816
ML_HEADS = 4
ML_DQK = D_MODEL // (2 * ML_HEADS)
ML_DV = D_MODEL // ML_HEADS
ML_QK = ML_HEADS * ML_DQK
ML_PROJ = 2 * ML_QK + 2 * D_MODEL + 4 * ML_HEADS
HEAD_DIM = 64
N_Q_HEADS = D_MODEL // HEAD_DIM
N_KV_HEADS = 4
GROUP = N_Q_HEADS // N_KV_HEADS
WINDOW = 128
BLOCK = 128
AT_PROJ = (N_Q_HEADS + 2 * N_KV_HEADS) * HEAD_DIM
MASK_VALUE = -1e30


def layer_norm(x, g, b):
    xf = x.astype(jnp.float32)
    mu = jnp.mean(xf, axis=-1, keepdims=True)
    var = jnp.mean(jnp.square(xf - mu), axis=-1, keepdims=True)
    return ((xf - mu) * lax.rsqrt(var + LN_EPS) * g + b).astype(x.dtype)

def swiglu_2(x, w_in, w_out):
    gu = x @ w_in
    g, u = gu[..., :D_FF], gu[..., D_FF:]
    return (jax.nn.silu(g) * u) @ w_out

def mlstm_chunkwise(q, k, v, i_pre, f_pre):
    B, H, S, dk = q.shape
    dv = v.shape[-1]
    nc = S // CHUNK
    q = q.astype(jnp.float32).reshape(B, H, nc, CHUNK, dk)
    k = k.astype(jnp.float32).reshape(B, H, nc, CHUNK, dk)
    v = v.astype(jnp.float32).reshape(B, H, nc, CHUNK, dv)
    logf = jax.nn.log_sigmoid(f_pre.astype(jnp.float32)).reshape(B, H, nc, CHUNK)
    ig = i_pre.astype(jnp.float32).reshape(B, H, nc, CHUNK)
    g = jnp.cumsum(logf, axis=-1)
    G = g[..., -1]
    w_end = G[..., None] - g + ig
    a = jnp.max(w_end, axis=-1)
    e_end = jnp.exp(w_end - a[..., None])
    K_c = jnp.einsum('bhcl,bhclv,bhclk->bhcvk', e_end, v, k)
    N_c = jnp.einsum('bhcl,bhclk->bhck', e_end, k)

    def step(carry, inp):
        C, n, m = carry
        Gc, ac, Kc, Nc = inp
        m_new = jnp.maximum(Gc + m, ac)
        sp = jnp.exp(Gc + m - m_new)
        sc = jnp.exp(ac - m_new)
        C_new = sp[..., None, None] * C + sc[..., None, None] * Kc
        n_new = sp[..., None] * n + sc[..., None] * Nc
        return (C_new, n_new, m_new), (C, n, m)

    init = (jnp.zeros((B, H, dv, dk), jnp.float32), jnp.zeros((B, H, dk), jnp.float32),
            jnp.zeros((B, H), jnp.float32))
    xs = (jnp.moveaxis(G, 2, 0), jnp.moveaxis(a, 2, 0), jnp.moveaxis(K_c, 2, 0), jnp.moveaxis(N_c, 2, 0))
    _, (C0, n0, m0) = lax.scan(step, init, xs)
    C0 = jnp.moveaxis(C0, 0, 2)
    n0 = jnp.moveaxis(n0, 0, 2)
    m0 = jnp.moveaxis(m0, 0, 2)

    tril = jnp.tril(jnp.ones((CHUNK, CHUNK), dtype=bool))
    dmat = g[..., :, None] - g[..., None, :] + ig[..., None, :]
    dmat = jnp.where(tril, dmat, MASK_VALUE)
    inter_log = g + m0[..., None]
    m_out = jnp.maximum(inter_log, jnp.max(dmat, axis=-1))
    wts = jnp.exp(dmat - m_out[..., None])
    s_inter = jnp.exp(inter_log - m_out)
    s_qk = jnp.einsum('bhcjd,bhcsd->bhcjs', q, k) * wts
    num = jnp.einsum('bhcjs,bhcsv->bhcjv', s_qk, v) + s_inter[..., None] * jnp.einsum('bhcvd,bhcjd->bhcjv', C0, q)
    den = jnp.sum(s_qk, axis=-1) + s_inter * jnp.einsum('bhcd,bhcjd->bhcj', n0, q)
    den = jnp.maximum(jnp.abs(den), jnp.exp(-m_out))
    h = num / den[..., None]
    return h.reshape(B, H, S, dv)

def mlstm_mixer(x, w_in, gate_b, norm_g, w_out):
    B, S, _ = x.shape
    p = x @ w_in
    q = p[..., :ML_QK].reshape(B, S, ML_HEADS, ML_DQK).transpose(0, 2, 1, 3)
    k = p[..., ML_QK:2 * ML_QK].reshape(B, S, ML_HEADS, ML_DQK).transpose(0, 2, 1, 3) * (ML_DQK ** -0.5)
    v = p[..., 2 * ML_QK:2 * ML_QK + D_MODEL].reshape(B, S, ML_HEADS, ML_DV).transpose(0, 2, 1, 3)
    o = p[..., 2 * ML_QK + D_MODEL:2 * ML_QK + 2 * D_MODEL]
    gates = (p[..., 2 * ML_QK + 2 * D_MODEL:] + gate_b).reshape(B, S, 4, ML_HEADS).transpose(2, 0, 3, 1)
    h_f = mlstm_chunkwise(q, k, v, gates[0], gates[1])
    flip = lambda a: jnp.flip(a, axis=2)
    h_b = flip(mlstm_chunkwise(flip(q), flip(k), flip(v), flip(gates[2]), flip(gates[3])))
    h = h_f + h_b
    mu = jnp.mean(h, axis=-1, keepdims=True)
    var = jnp.mean(jnp.square(h - mu), axis=-1, keepdims=True)
    h = (h - mu) * lax.rsqrt(var + LN_EPS)
    h = h.transpose(0, 2, 1, 3).reshape(B, S, D_MODEL) * norm_g
    out = jax.nn.sigmoid(o.astype(jnp.float32)) * h
    return out.astype(x.dtype) @ w_out

def alibi_slopes():
    return jnp.exp2(-8.0 * jnp.arange(1, N_Q_HEADS + 1, dtype=jnp.float32) / N_Q_HEADS)

def window_attention(x, w_in, sink, w_out):
    B, S, _ = x.shape
    nb = S // BLOCK
    p = x @ w_in
    nq = N_Q_HEADS * HEAD_DIM
    nk = N_KV_HEADS * HEAD_DIM
    q = p[..., :nq].reshape(B, nb, BLOCK, N_KV_HEADS, GROUP, HEAD_DIM)
    k = p[..., nq:nq + nk].reshape(B, S, N_KV_HEADS, HEAD_DIM)
    v = p[..., nq + nk:].reshape(B, S, N_KV_HEADS, HEAD_DIM)
    pad = ((0, 0), (BLOCK, BLOCK), (0, 0), (0, 0))
    kp = jnp.pad(k, pad).reshape(B, nb + 2, BLOCK, N_KV_HEADS, HEAD_DIM)
    vp = jnp.pad(v, pad).reshape(B, nb + 2, BLOCK, N_KV_HEADS, HEAD_DIM)
    kw = jnp.concatenate([kp[:, :-2], kp[:, 1:-1], kp[:, 2:]], axis=2)
    vw = jnp.concatenate([vp[:, :-2], vp[:, 1:-1], vp[:, 2:]], axis=2)
    s = jnp.einsum('bnqkgd,bnskd->bnkgqs', q, kw).astype(jnp.float32) * (HEAD_DIM ** -0.5)
    qi = jnp.arange(BLOCK)[:, None]
    kj = jnp.arange(3 * BLOCK)[None, :]
    rel = qi - kj + BLOCK
    dist = jnp.abs(rel).astype(jnp.float32)
    key_pos = jnp.arange(nb)[:, None] * BLOCK - BLOCK + jnp.arange(3 * BLOCK)[None, :]
    valid = (jnp.abs(rel) <= WINDOW)[None] & ((key_pos >= 0) & (key_pos < S))[:, None, :]
    slopes = alibi_slopes().reshape(N_KV_HEADS, GROUP)
    s = s - slopes[:, :, None, None] * dist
    s = jnp.where(valid[None, :, None, None], s, MASK_VALUE)
    sink_l = sink.astype(jnp.float32).reshape(N_KV_HEADS, GROUP)[None, None, :, :, None, None]
    m = jnp.maximum(jnp.max(s, axis=-1, keepdims=True), sink_l)
    pe = jnp.exp(s - m)
    attn = pe / (jnp.sum(pe, axis=-1, keepdims=True) + jnp.exp(sink_l - m))
    o = jnp.einsum('bnkgqs,bnskd->bnqkgd', attn, vw.astype(jnp.float32)).reshape(B, S, nq)
    return o.astype(x.dtype) @ w_out

def second_inputs(seed: int = 0) -> dict:
    key = jax.random.key(seed)
    ks = jax.random.split(key, 16)
    nrm = jax.random.normal
    x = nrm(ks[0], (BATCH, SEQ, D_MODEL), jnp.float32)
    ffn_w_in = nrm(ks[1], (DEPTH, 2, D_MODEL, 2 * D_FF), jnp.float32) * D_MODEL ** -0.5
    ffn_w_out = nrm(ks[2], (DEPTH, 2, D_FF, D_MODEL), jnp.float32) * (D_FF ** -0.5 * BETA)
    ln_g = 1.0 + 0.02 * nrm(ks[3], (DEPTH, 3, D_MODEL), jnp.float32)
    ln_b = 0.02 * nrm(ks[4], (DEPTH, 3, D_MODEL), jnp.float32)
    ml_w_in = nrm(ks[5], (N_A, D_MODEL, ML_PROJ), jnp.float32) * D_MODEL ** -0.5
    ml_w_in = ml_w_in.at[..., 2 * ML_QK:2 * ML_QK + D_MODEL].multiply(BETA)
    f_off = jnp.linspace(3.0, 6.0, ML_HEADS, dtype=jnp.float32)
    zero = jnp.zeros((ML_HEADS,), jnp.float32)
    gate_off = jnp.stack([zero, f_off, zero, f_off])
    ml_gate_b = (0.1 * nrm(ks[6], (N_A, 4, ML_HEADS), jnp.float32) + gate_off).reshape(N_A, 4 * ML_HEADS)
    ml_norm_g = 1.0 + 0.02 * nrm(ks[7], (N_A, D_MODEL), jnp.float32)
    ml_w_out = nrm(ks[8], (N_A, D_MODEL, D_MODEL), jnp.float32) * (D_MODEL ** -0.5 * BETA)
    at_w_in = nrm(ks[9], (N_B, D_MODEL, AT_PROJ), jnp.float32) * D_MODEL ** -0.5
    at_w_in = at_w_in.at[..., (N_Q_HEADS + N_KV_HEADS) * HEAD_DIM:].multiply(BETA)
    at_sink = 0.5 * nrm(ks[10], (N_B, N_Q_HEADS), jnp.float32)
    at_w_out = nrm(ks[11], (N_B, D_MODEL, D_MODEL), jnp.float32) * (D_MODEL ** -0.5 * BETA)
    return {"x": x, "ffn_w_in": ffn_w_in, "ffn_w_out": ffn_w_out, "ln_g": ln_g, "ln_b": ln_b,
            "ml_w_in": ml_w_in, "ml_gate_b": ml_gate_b, "ml_norm_g": ml_norm_g, "ml_w_out": ml_w_out,
            "at_w_in": at_w_in, "at_sink": at_sink, "at_w_out": at_w_out}

def second_block(x, ffn_w_in, ffn_w_out, ln_g, ln_b, ml_w_in, ml_gate_b, ml_norm_g, ml_w_out,
              at_w_in, at_sink, at_w_out):
    for l in range(DEPTH):
        x = layer_norm(ALPHA * x + 0.5 * swiglu_2(x, ffn_w_in[l, 0], ffn_w_out[l, 0]), ln_g[l, 0], ln_b[l, 0])
        j = l // N_MIXERS
        if l % N_MIXERS == 0:
            y = mlstm_mixer(x, ml_w_in[j], ml_gate_b[j], ml_norm_g[j], ml_w_out[j])
        else:
            y = window_attention(x, at_w_in[j], at_sink[j], at_w_out[j])
        x = layer_norm(ALPHA * x + y, ln_g[l, 1], ln_b[l, 1])
        x = layer_norm(ALPHA * x + 0.5 * swiglu_2(x, ffn_w_in[l, 1], ffn_w_out[l, 1]), ln_g[l, 2], ln_b[l, 2])
    return x


def setup_inputs(seed=0):
    out = dict(first_inputs(seed))
    for name, value in second_inputs(seed + 1).items():
        if name != "x":
            out[name + "_2"] = value
    return out


def reference(
    x, positions, norm_mix, ev_w_in, ev_conv_w, ev_conv_b, ev_dt_bias, ev_a_log, ev_d_skip,
    ev_gate_norm, ev_lambdas, ev_subln, ev_w_out, od_w_in, od_lam_re, od_lam_im, od_log_step,
    od_b_re, od_b_im, od_c_re, od_c_im, od_d_skip, od_w_glu, od_b_glu, od_q_norm, od_w_uq,
    od_kv_norm, od_w_ukv, od_w_out, norm_ffn, ffn_gate, ffn_up, ffn_down, norm_final,
    ffn_w_in_2, ffn_w_out_2, ln_g_2, ln_b_2, ml_w_in_2, ml_gate_b_2, ml_norm_g_2, ml_w_out_2,
    at_w_in_2, at_sink_2, at_w_out_2,
):
    x = first_block(
        x, positions, norm_mix, ev_w_in, ev_conv_w, ev_conv_b, ev_dt_bias, ev_a_log, ev_d_skip,
        ev_gate_norm, ev_lambdas, ev_subln, ev_w_out, od_w_in, od_lam_re, od_lam_im,
        od_log_step, od_b_re, od_b_im, od_c_re, od_c_im, od_d_skip, od_w_glu, od_b_glu,
        od_q_norm, od_w_uq, od_kv_norm, od_w_ukv, od_w_out, norm_ffn, ffn_gate, ffn_up,
        ffn_down, norm_final,
    )
    return second_block(
        x, ffn_w_in_2, ffn_w_out_2, ln_g_2, ln_b_2, ml_w_in_2, ml_gate_b_2, ml_norm_g_2,
        ml_w_out_2, at_w_in_2, at_sink_2, at_w_out_2,
    )


_drawn_inputs = setup_inputs


def setup_inputs(seed=0):
    import zlib

    import numpy as np

    out = dict(_drawn_inputs(seed))
    spreads = {}
    factors = {'norm_mix': 3.674,
     'ev_conv_b': 5.399,
     'ev_d_skip': 171.201,
     'ev_gate_norm': 8.0,
     'ev_subln': 8.0,
     'od_lam_re': 64.0,
     'od_lam_im': 30.152,
     'od_log_step': 33.616,
     'od_b_re': 38.72,
     'od_b_im': 43.4,
     'od_c_re': 42.688,
     'od_c_im': 43.248,
     'od_d_skip': 22.49,
     'od_b_glu': 64.0,
     'od_q_norm': 8.0,
     'od_kv_norm': 8.0,
     'norm_ffn': 6.145,
     'norm_final': 4.92,
     'ml_norm_g_2': 73.6,
     'at_sink_2': 29.227}
    for name, (base, spread) in spreads.items():
        noise = np.random.default_rng([zlib.crc32(name.encode()), seed]).standard_normal(out[name].shape)
        drawn = base * np.exp(spread * noise) if base else spread * noise
        out[name] = jnp.asarray(drawn.astype(out[name].dtype))
    for name, factor in factors.items():
        out[name] = (out[name] * factor).astype(out[name].dtype)
    return out
```

```python
import concourse.bass as bass
from concourse import mybir
from contextlib import ExitStack

F32 = mybir.dt.float32
F32R = mybir.dt.float32r
I32 = mybir.dt.int32
ALU = mybir.AluOpType
ACT = mybir.ActivationFunctionType
AX = mybir.AxisListType

P = 128
T = 512
TT = T // P
D = 1024
KD = D // P
FF = 2816
KF = FF // P
SLOT = 2048
RMS_EPS = 1e-6
LN_EPS = 1e-5
ALPHA = 4 ** 0.25


class Own:

    def __init__(self, eng, sems, steps, **begin):
        self.eng, self.sems, self.steps = eng, dict(sems), steps
        self.n = dict.fromkeys(sems, 0)
        for name, n in begin.items():
            eng.sem_inc(sems[name], n)
            self.n[name] = n

    def knows(self, sems):
        self.sems.update(sems)
        self.n.update(dict.fromkeys(sems, 0))

    def __call__(self, ins, name=None, wait=True):
        name = name or self.steps
        ins.then_inc(self.sems[name], 1)
        self.n[name] = self.n[name] + 1
        if wait:
            self.eng.wait_ge(self.sems[name], self.n[name])

    def loop(self, iters, body, **per):
        base = dict(self.n)
        with self.eng.Fori(0, iters) as i:
            for name, n in per.items():
                self.n[name] = i * n + base[name]
            body(i)
        for name in self.n:
            self.n[name] = base[name] + iters * per.get(name, 0)


def build(nc, io, plan):
    ctx = ExitStack()
    with ctx:
        here = [16512]

        def sb(name, shape, dt=F32, at=None):
            size = 4
            for s in shape[1:]:
                size *= s
            size = (size + 31) // 32 * 32
            off = here[0] if at is None else at
            if at is None:
                here[0] += size
            return nc.alloc_sbuf_tensor_at(name, shape, dt, offset=off)

        def sem(name):
            return ctx.enter_context(nc.semaphore(name))

        ps = ctx.enter_context(nc.psum_tensor("ps", [P, 8, 512], F32))
        R = sb("R", [P, KD, T])
        XH_AT = here[0]
        XH = sb("XH", [P, KD, T], F32R)
        XL = sb("XL", [P, KD, T], F32R)
        RAW = sb("RAW", [P, 2, SLOT])
        WH = sb("WH", [P, 2, SLOT], F32R)
        WL = sb("WL", [P, 2, SLOT], F32R)
        WORK = here[0]
        HH = sb("HH", [P, KF, T], F32R)
        HL = sb("HL", [P, KF, T], F32R)
        WORK2 = here[0]
        S1 = sb("S1", [P, T])
        S2 = sb("S2", [P, T])
        SQ = sb("SQ", [P, 2, T])
        TH = sb("TH", [P, 2, T])
        SG = sb("SG", [P, 2, T])
        HV = sb("HV", [P, 2, T])
        CONST = here[0]
        XIN = sb("XIN", [P, TT, D], at=WORK)
        OUT = sb("OUT", [P, TT, D], at=WORK)
        ident = sb("ident", [P, P])
        ones = sb("ones", [P, P])
        VROW = sb("VROW", [P, 2, P], at=WORK2)
        VEC = sb("VEC", [P, 2 * P])
        stat = sb("stat", [P, 12, 4])
        sb_small = sb("small", [P, 58])
        sb_w2 = sb("turn", [P, 2, 16])
        DG = sb("DG", [P, 2, T], at=WORK2 + 8 * T * 4)
        XT = sb("XT", [P, 2, T], at=WORK2 + 4 * T * 4)

        raw_in = [sem("raw_in0"), sem("raw_in1")]
        names = """raw_free split_ready unit_done passed const_ready vrow_in vec_ready vec_copied dve_steps pool_steps act_steps
        gate_taken tanh_ready hv_ready hh_ready h_ready r_ready sq_ready s1_added s2_added stats_ready diag_ready
        bcast_ready t_ready xh_ready x_ready x_in xt_ready out_t out_ev out_done x_in_right norm_r""".split()
        S = {n: sem(n) for n in names}
        block = ctx.enter_context(nc.Block())
        vec_col = {}
        vrows = []

        def add_vec(name, ap, rows):
            n0 = sum(r for _, r, _ in vrows)
            used = n0 % P
            if used + rows > P:
                vrows.append((None, P - used, None))
                n0 += P - used
            vrows.append((ap, rows, n0))
            vec_col[name] = n0

        def v1(name, ap2):
            a, m = ap2.shape
            add_vec(name, ap2.rearrange("a (n p) -> (a n) p", p=P), a * m // P)

        v1("norm_mix", io["norm_mix"])
        v1("norm_ffn", io["norm_ffn"])
        add_vec("norm_final", io["norm_final"].rearrange("(n p) -> n p", p=P), 8)
        v1("ln_g", io["ln_g_2"].rearrange("a b c -> (a b) c"))
        v1("gate_norm", io["ev_gate_norm"])
        v1("subln", io["ev_subln"])
        v1("s5_skip", io["od_d_skip"])
        v1("b_glu", io["od_b_glu"])
        v1("q_norm", io["od_q_norm"])
        v1("kv_norm", io["od_kv_norm"])
        v1("ml_norm", io["ml_norm_g_2"])
        v1("ln_b", io["ln_b_2"].rearrange("a b c -> (a b) c"))
        v1("conv_w", io["ev_conv_w"].rearrange("a b c -> (a b) c"))
        v1("conv_b", io["ev_conv_b"])

        def vec_pages():
            n = sum(r for _, r, _ in vrows)
            last = vrows[0][1]
            for ap, r, n0 in vrows:
                if ap is not None and n0 < P:
                    last = n0 + r
            return [(0, min(last, P)), (P, n)] if n > P else [(0, n)]

        def vcol(name, k):
            c = vec_col[name] + k
            return VEC[:, c:c + 1]

        groups = []
        total = [0]

        def units(iters, parts):
            n0 = total[0]
            assert iters == 1 or len(parts) % 2 == 0
            groups.append((n0, iters, parts))
            total[0] += iters * len(parts)
            return n0

        st = []
        p_count = 0
        c_count = 0
        s1_count = 0
        dg_count = 0
        nr_count = 0
        acc = -1
        f_count = 0
        x_extra = 0
        for s in plan:
            e = dict(s)
            if s["kind"] == "ffn":
                g, u, d = s["gate"], s["up"], s["down"]
                e["n0"] = units(11, [(g[0], 0, 8, g[1], 256, 256), (u[0], 0, 8, u[1], 256, 256)])
                e["nd"] = units(8, [(d, 0, 11, 0, P, P), (d, 11, 22, 0, P, P)])
                e["f"], e["p"] = f_count, p_count
                f_count += 1
                p_count += 1
                acc += 1
                e["a"], e["x"] = acc, c_count + x_extra - 1
                e["s1"] = s["mean"]
            elif s["kind"] == "norm":
                e["c"], e["a"], e["dg_at"], e["x"] = c_count, acc, dg_count, c_count + x_extra
                e["s1_at"] = s1_count - 8
                c_count += 1
                dg_count += 2 if e["ln"] else 1
                if e["ln"] or e["keep"]:
                    nr_count += 8
            elif s["kind"] == "load":
                acc += 1
                e["a"], e["p"], e["s1"] = acc, p_count, s["mean"]
                p_count += 1
            elif s["kind"] == "ev_attn":
                w, wo = s["w_in"], s["w_out"]
                e["x"] = c_count + x_extra - 1
                e["nv"] = units(1, [(w, 4 * g, 4 * g + 4, 4624 + 512 * h, 0, 512) for h in range(2) for g in range(2)])
                e["nq"] = units(1, [(w, 0, 8, 2576 + 256 * u, 0, 256) for u in range(8)])
                e["no"] = units(1, [(wo, 8, 16, 256 * u, 0, 256) for u in range(4)])
                e["p"], e["a"], e["s1"] = p_count, None, False
                p_count += 1
            elif s["kind"] == "ev_mamba":
                w, wo = s["w_in"], s["w_out"]
                e["x"] = c_count + x_extra - 1
                e["nd"] = units(1, [(w, 0, 8, 2560, 0, 16, P)])
                e["nx"] = units(1, [(w, 0, 8, 1024 + 256 * u, 0, 256) for u in (4, 5, 0, 1, 2, 3)])
                e["nz"] = units(1, [(w, 0, 8, 256 * u, 0, 256) for u in range(4)])
                e["no"] = units(1, [(wo, 0, 8, 256 * u, 0, 256) for u in range(4)])
                acc += 1
                x_extra += 1
                e["p"], e["a"], e["s1"] = p_count, acc, False
                p_count += 1
            elif s["kind"] == "win":
                w, wo = s["w_in"], s["w_out"]
                e["x"] = c_count + x_extra - 1
                e["nv"] = units(1, [(w, 0, 8, 1280, 0, 256), (w, 0, 8, 1024, 0, 256)] + [(w, 0, 8, 256 * u, 0, 256) for u in range(4)])
                e["no"] = units(1, [(wo, 0, 8, 256 * u, 0, 256) for u in range(4)])
                acc += 1
                e["p"], e["a"], e["s1"] = p_count, acc, True
                p_count += 1
            elif s["kind"] == "mlstm":
                w, wo = s["w_in"], s["w_out"]
                e["x"] = c_count + x_extra - 1
                values = [[(w, 4 * g, 4 * g + 4, 1024 + 512 * h, 0, 512) for g in range(2)] for h in range(2)]
                e["n0"] = units(1, values[0] + [(w, 0, 8, 3072, 0, 16, P)] + values[1]
                                + [(w, 0, 8, c + 256 * u, 0, 256) for c in (0, 2048) for u in range(4)]
                                + [(wo, 0, 8, 256 * u, 0, 256) for u in range(4)])
                acc += 1
                x_extra += 1
                e["p"], e["a"], e["s1"] = p_count, acc, True
                p_count += 1
            elif s["kind"] == "od":
                w, wo = s["w_in"], s["w_out"]
                e["x"] = c_count + x_extra - 1
                e["nu"] = units(1, [(w, 0, 8, 0, 0, 256), (w, 0, 8, 256, 0, 256), (w, 0, 8, 512, 0, 256), (w, 0, 8, 768, 0, P),
                                    (w, 0, 8, 896, 0, 256), (w, 0, 8, 1152, 0, 32, P, 64)]
                                + [(s["uq"], 0, 3, 384 * g, 0, 384) for g in range(2)]
                                + [(s["ukv"], 0, 2, 0, 0, 1024), (s["glu"], 0, 4, 0, 0, 512)]
                                + [(wo, 0, 8, 256 * u, 0, 256) for u in range(4)])
                e["table_at"], e["pool_at"] = (e["nu"] + 8) // 2 * 2, (e["nu"] + 11) // 2 * 2
                acc += 1
                e["p"], e["a"], e["s1"] = p_count, acc, False
                p_count += 1
            e["nr_at"], e["p_end"] = nr_count, p_count
            if e.get("s1"):
                e["s1_at"] = s1_count
                s1_count += 8
            st.append(e)
        if total[0] % 2:
            units(1, [groups[0][2][0]])

        @block.sync
        def _(sp):
            for ap, rows, n0 in vrows:
                if ap is not None:
                    sp.dma_start(VROW[n0 % P:n0 % P + rows, n0 // P, :], ap).then_inc(S["vrow_in"], 16)
            for n0, iters, parts in groups:
                def emit(i):
                    for s, (v, k0, k1, c0, cs, w, *more) in enumerate(parts):
                        n = n0 + s
                        slot = n % 2
                        pitch, at = (more + [0])[0:2] if more else (w, 0)
                        dst = RAW[:, slot, 0:(k1 - k0) * pitch].rearrange("p (k n) -> p k n", n=pitch)[:, :, at:at + w]
                        sp.wait_ge(S["raw_free"], i * len(parts) + (n + 1))
                        sp.sem_inc(S["passed"], 1)
                        sp.dma_start(dst, v[:, k0:k1, bass.ds(i * cs + c0, w)]).then_inc(raw_in[slot], 16)
                if iters > 1:
                    with sp.Fori(0, iters) as i:
                        emit(i)
                else:
                    emit(0)
            sp.wait_ge(S["out_ev"], 2 * TT)
            sp.dma_start(io["out"].rearrange("b (j p) n -> p (b j) n", p=P), OUT[:]).then_inc(S["out_done"], 16)
            sp.wait_ge(S["out_done"], 16)

        def unit_done_at(n):
            return n + 3

        mixers = {}

        def mm(out, lhsT, rhs, start=True, stop=True, **kw):
            return nc.tensor.matmul(out, lhsT, rhs, start=start, stop=stop, **kw)

        def pe_three(out, wh, wl, xh, xl, start, stop):
            nc.tensor.matmul(out, wh, xh, start=start, stop=False)
            nc.tensor.matmul(out, wh, xl, start=False, stop=False)
            return nc.tensor.matmul(out, wl, xh, start=False, stop=stop)

        def fm_unit(pe, n, slot, outs, xh, xl, kts, w, start=True, stop=True, x_at=None, wait_k=None, rows=P):
            pe.wait_ge(S["split_ready"], n + 1)
            for q, k in enumerate(kts):
                if x_at is not None:
                    pe.wait_ge(S["x_ready"], x_at + k + 1)
                if wait_k is not None:
                    wait_k(k)
                for o, c in outs:
                    ws = slice(q * w + c, q * w + c + rows)
                    last = pe_three(o, WH[:, slot, ws], WL[:, slot, ws], xh(k), xl(k),
                                    start and q == 0, stop and q == len(kts) - 1)
            last.then_inc(S["unit_done"], 1)

        XHk = lambda k: XH[:, k, :]
        XLk = lambda k: XL[:, k, :]

        def ffn_pe(pe, e):
            f, n0, nd, x_at = e["f"], e["n0"], e["nd"], 8 * e["x"]
            pe.wait_ge(S["gate_taken"], 22 * f + 1)
            pe.wait_ge(S["hv_ready"], 22 * f + 1)
            for u in range(2):
                pe.wait_ge(S["split_ready"], n0 + u + 1)
            for k in range(KD):
                pe.wait_ge(S["x_ready"], x_at + k + 1)
                for u in range(2):
                    for t in range(2):
                        ws = slice(k * 256 + t * P, k * 256 + t * P + P)
                        last = pe_three(ps[:, 2 * u + t, :], WH[:, (n0 + u) % 2, ws], WL[:, (n0 + u) % 2, ws], XHk(k), XLk(k),
                                        k == 0, k == KD - 1)
                    if k == KD - 1:
                        last.then_inc(S["unit_done"], 1)
            with pe.Fori(0, 10) as i:
                pe.wait_ge(S["gate_taken"], i * 2 + (22 * f + 3))
                fm_unit(pe, i * 2 + (n0 + 2), n0 % 2, [(ps[:, 0, :], 0), (ps[:, 1, :], P)], XHk, XLk, range(8), 256)
                pe.wait_ge(S["hv_ready"], i * 2 + (22 * f + 3))
                fm_unit(pe, i * 2 + (n0 + 3), (n0 + 1) % 2, [(ps[:, 2, :], 0), (ps[:, 3, :], P)], XHk, XLk, range(8), 256)
            with pe.Fori(0, 4) as i:
                for t in range(2):
                    pe.wait_ge(S["r_ready"], i * 2 + (8 * e["p"] + t + 1))
                    pe.wait_ge(S["h_ready"], 22 * f + 11)
                    fm_unit(pe, i * 4 + (nd + 2 * t), nd % 2, [(ps[:, 4 + t, :], 0)], lambda k: HH[:, k, :],
                            lambda k: HL[:, k, :], range(11), P, stop=False)
                    pe.wait_ge(S["h_ready"], 22 * f + 22)
                    fm_unit(pe, i * 4 + (nd + 2 * t + 1), (nd + 1) % 2, [(ps[:, 4 + t, :], 0)], lambda k: HH[:, k, :],
                            lambda k: HL[:, k, :], range(11, 22), P, start=False)

        def norm_pe(pe, e):
            c, ln = e["c"], e["ln"]
            if ln:
                pe.wait_ge(S["s1_added"], e["s1_at"] + 8)
                for t in range(TT):
                    mm(ps[:, 6, 4 + t:5 + t], S1[:, t * P:(t + 1) * P], ones[:, 0:1])
            pe.wait_ge(S["s2_added"], 8 * e["a"] + 10)
            for t in range(TT):
                last = mm(ps[:, 6, t:t + 1], S2[:, t * P:(t + 1) * P], ones[:, 0:1])
            last.then_inc(S["stats_ready"], 1)
            pe.wait_ge(S["diag_ready"], e["dg_at"] + 1)
            nc.tensor.matmul(ps[:, 7, :], ones[:], DG[:, 0, :], start=True, stop=True).then_inc(S["bcast_ready"], 1)
            if ln:
                pe.wait_ge(S["diag_ready"], e["dg_at"] + 2)
                nc.tensor.matmul(ps[:, 6, :], ones[:], DG[:, 1, :], start=True, stop=True).then_inc(S["bcast_ready"], 1)

        def square_act(act, e):
            for k in range(KD):
                act.wait_ge(S["r_ready"], 8 * e["p"] + 3 + k)
                act.wait_ge(S["s2_added"], 8 * e["a"] + k + 1)
                nc.scalar.activation(SQ[:, k % 2, :], R[:, k, :], ACT.Square).then_inc(S["sq_ready"], 1)

        for kind, make in MIXERS.items():
            if any(e["kind"] == kind for e in st):
                mixers[kind] = make(nc, dict(locals(), Own=Own))

        @block.gpsimd
        def _(pool):
            own = Own(pool, S, "pool_steps")
            own(nc.gpsimd.memset(ident[:], 0.0))
            nc.gpsimd.affine_select(out=ident[:], in_=ident[:], compare_op=ALU.not_equal, fill=1.0, base=0,
                                    pattern=[[-1, P]], channel_multiplier=1).then_inc(S["const_ready"], 1)
            nc.gpsimd.memset(ones[:], 1.0).then_inc(S["const_ready"], 1)
            own(nc.gpsimd.memset(RAW[:], 0.0))
            pool.sem_inc(S["raw_free"], 2)

            def split_units(a, z):
                if a == z:
                    return
                base = own.n["pool_steps"]
                with pool.Fori(0, (z - a) // 2) as i:
                    for s in range(2):
                        pool.wait_ge(S["unit_done"], i * 2 + (a + s + 1))
                        pool.sem_inc(S["passed"], 1)
                        pool.wait_ge(raw_in[s], i * 16 + (8 * a + 16))
                        pool.sem_inc(S["passed"], 1)
                        nc.gpsimd.tensor_scalar(WH[:, s, :], RAW[:, s, :], 1.0, 0.0, ALU.mult, ALU.add)\
                            .then_inc(S["pool_steps"], 1)
                        pool.wait_ge(S["pool_steps"], i * 2 + (base + s + 1))
                        nc.gpsimd.tensor_tensor(WL[:, s, :], RAW[:, s, :], WH[:, s, :].bitcast(F32), ALU.subtract)\
                            .then_inc(S["split_ready"], 1)
                        pool.wait_ge(S["split_ready"], i * 2 + (a + s + 1))
                        pool.sem_inc(S["raw_free"], 1)
                own.n["pool_steps"] += z - a

            done = 0
            for e in st:
                if "pool" in mixers.get(e["kind"], {}):
                    mixers[e["kind"]]["pool"](pool, own, e, split_units, done)
                    done = e["pool_at"]
            split_units(done, total[0])

        @block.tensor
        def _(pe):
            pe.sem_inc(S["unit_done"], 2)
            pe.wait_ge(S["const_ready"], 2)
            pe.wait_ge(S["vrow_in"], 16 * sum(ap is not None for ap, _, _ in vrows))
            for a, b in vec_pages():
                last = nc.tensor.transpose(ps[:, 6, a:b], VROW[0:b - a, a // P, :], ident[0:b - a, 0:b - a])
            last.then_inc(S["vec_ready"], 1)

            def load(e):
                for k in range(KD):
                    pe.wait_ge(S["x_in_right" if k >= 4 else "x_in"], 16)
                    pe.wait_ge(S["r_ready"], k + 1)
                    for j in range(TT):
                        last = nc.tensor.transpose(ps[:, 4 + k % 2, j * P:(j + 1) * P], XIN[:, j, k * P:(k + 1) * P], ident[:])
                    last.then_inc(S["xt_ready"], 1)

            def store(e):
                for q in range(2 * TT):
                    j, h = q // 2, q % 2
                    if e["nr_at"]:
                        pe.wait_ge(S["norm_r"], e["nr_at"])
                    pe.wait_ge(S["r_ready"], 8 * e["p_end"] + 2)
                    if q >= 2:
                        pe.wait_ge(S["out_ev"], q - 1)
                    for k in range(4):
                        last = nc.tensor.transpose(ps[:, q % 2, k * P:(k + 1) * P], R[:, 4 * h + k, j * P:(j + 1) * P], ident[:])
                    last.then_inc(S["out_t"], 1)

            stages = dict(load=load, store=store, norm=lambda e: norm_pe(pe, e), ffn=lambda e: ffn_pe(pe, e),
                          **{k: (lambda m: lambda e: m["pe"](pe, e))(m) for k, m in mixers.items()})
            for e in st:
                stages[e["kind"]](e)

        @block.scalar
        def _(act):
            for h in range(2):
                act.dma_start(XIN[:, :, 512 * h:512 * h + 512],
                              io["x"].rearrange("b (j p) n -> p (b j) n", p=P)[:, :, 512 * h:512 * h + 512])\
                    .then_inc(S["x_in_right" if h else "x_in"], 16)
            act.wait_ge(S["vec_copied"], 1)
            own = Own(act, S, "act_steps")
            for e in st:
                if e["kind"] in mixers:
                    mixers[e["kind"]]["act"](act, own, e)
                elif e["kind"] == "load":
                    for k in range(KD):
                        act.wait_ge(S["r_ready"], 8 * e["p"] + 3 + k)
                        act.wait_ge(S["s2_added"], 8 * e["a"] + k + 1)
                        nc.scalar.activation(SQ[:, k % 2, :], R[:, k, :], ACT.Square).then_inc(S["sq_ready"], 1)
                elif e["kind"] == "ffn":
                    f, n0 = e["f"], e["n0"]
                    with act.Fori(0, 11) as i:
                        act.wait_ge(S["unit_done"], i * 2 + unit_done_at(n0))
                        for t in range(2):
                            nc.scalar.activation(TH[:, t, :], ps[:, t, :], ACT.Tanh, scale=0.5).then_inc(S["tanh_ready"], 1)
                        for t in range(2):
                            act.wait_ge(S["hv_ready"], i * 2 + (22 * f + 2 + t))
                            nc.scalar.activation(HH[:, bass.ds(i * 2 + t, 1), :].rearrange("p a n -> p (a n)"), HV[:, t, :],
                                                 ACT.Copy).then_inc(S["hh_ready"], 1)
                    with act.Fori(0, 4) as i:
                        for t in range(2):
                            act.wait_ge(S["r_ready"], i * 2 + (8 * e["p"] + 3 + t))
                            act.wait_ge(S["s2_added"], i * 2 + (8 * e["a"] + t + 1))
                            nc.scalar.activation(SQ[:, t, :], R[:, bass.ds(i * 2 + t, 1), :].rearrange("p a n -> p (a n)"),
                                                 ACT.Square).then_inc(S["sq_ready"], 1)
                elif e["kind"] == "norm":
                    for k in range(KD):
                        act.wait_ge(S["t_ready"], 8 * e["c"] + k + 1)
                        g = vcol(e["gain"][0], e["gain"][1] * 8 + k)
                        if e["ln"] or e["keep"]:
                            b = vcol(e["bias"][0], e["bias"][1] * 8 + k) if e["ln"] else 0.0
                            nc.scalar.activation(R[:, k, :], XT[:, k % 2, :], ACT.Identity, scale=g, bias=b).then_inc(S["norm_r"], 1)
                            nc.scalar.activation(XH[:, k, :], XT[:, k % 2, :], ACT.Identity, scale=g, bias=b).then_inc(S["xh_ready"], 1)
                        else:
                            nc.scalar.activation(XH[:, k, :], XT[:, k % 2, :], ACT.Identity, scale=g).then_inc(S["xh_ready"], 1)
                elif e["kind"] == "store":
                    for q in range(2 * TT):
                        j, h = q // 2, q % 2
                        act.wait_ge(S["out_t"], q + 1)
                        nc.scalar.activation(OUT[:, j, h * 512:(h + 1) * 512], ps[:, q % 2, :], ACT.Copy).then_inc(S["out_ev"], 1)

        @block.vector
        def _(dve):
            v = nc.vector
            own = Own(dve, S, "dve_steps", gate_taken=1, hv_ready=1, r_ready=2, s2_added=2)
            dve.wait_ge(S["vec_ready"], 1)
            for n, (a, b) in enumerate(vec_pages()):
                own(v.tensor_copy(VEC[:, a:b], ps[:, 6, a:b]))
            own(v.memset(S1[:], 0.0), "vec_copied")
            own(v.memset(S2[:], 0.0))

            def sums(e, at, rk, sq):
                if e["s1"]:
                    own(v.tensor_tensor(S1[:], S1[:], rk, ALU.add), "s1_added")
                dve.wait_ge(S["sq_ready"], at + 1)
                own(v.tensor_tensor(S2[:], S2[:], sq, ALU.add), "s2_added")

            def residual(e, i, t, per, bank, unit):
                rk = R[:, bass.ds(i * per + t, 1), :].rearrange("p a n -> p (a n)")
                dve.wait_ge(S["unit_done"], unit)
                own(v.scalar_tensor_tensor(rk, rk, e["alpha"], ps[:, bank, :], ALU.mult, ALU.add), "r_ready")
                if e["a"] is not None:
                    sums(e, i * per + (8 * e["a"] + t), rk, SQ[:, t % 2, :])

            def load(e):
                for k in range(KD):
                    dve.wait_ge(S["xt_ready"], k + 1)
                    own(v.tensor_copy(R[:, k, :], ps[:, 4 + k % 2, :]), "r_ready")
                    sums(e, 8 * e["a"] + k, R[:, k, :], SQ[:, k % 2, :])

            def ffn(e):
                f, n0, nd = e["f"], e["n0"], e["nd"]

                def up(i):
                    for t in range(2):
                        dve.wait_ge(S["tanh_ready"], i * 2 + (22 * f + t + 1))
                        own(v.scalar_tensor_tensor(SG[:, t, :], TH[:, t, :], 1.0, ps[:, t, :], ALU.add, ALU.mult), "gate_taken")
                    dve.wait_ge(S["unit_done"], i * 2 + unit_done_at(n0 + 1))
                    for t in range(2):
                        own(v.scalar_tensor_tensor(HV[:, t, :], SG[:, t, :], e["half"], ps[:, 2 + t, :], ALU.mult, ALU.mult), "hv_ready")
                    for t in range(2):
                        dve.wait_ge(S["hh_ready"], i * 2 + (22 * f + t + 1))
                        hj = lambda h: h[:, bass.ds(i * 2 + t, 1), :].rearrange("p a n -> p (a n)")
                        own(v.tensor_tensor(hj(HL), HV[:, t, :], hj(HH).bitcast(F32), ALU.subtract), "h_ready")

                own.loop(11, up, gate_taken=2, hv_ready=2, h_ready=2)

                def down(i):
                    for t in range(2):
                        residual(e, i, t, 2, 4 + t, i * 4 + unit_done_at(nd + 2 * t + 1))

                own.loop(4, down, r_ready=2, s2_added=2, **({"s1_added": 2} if e["s1"] else {}))

            def norm(e):
                ln = e["ln"]
                dve.wait_ge(S["stats_ready"], e["c"] + 1)
                MU, MS, VAR, Y, A, B, NB = (stat[:, q, :] for q in range(7))
                if ln:
                    own(v.tensor_scalar(MU, ps[:, 6, 4:8], 1.0 / D, None, ALU.mult), wait=False)
                    own(v.tensor_scalar(MS, ps[:, 6, 0:4], 1.0 / D, LN_EPS, ALU.mult, ALU.add))
                    own(v.tensor_tensor(A, MU, MU, ALU.mult))
                    own(v.tensor_tensor(VAR, MS, A, ALU.subtract))
                else:
                    own(v.tensor_scalar(VAR, ps[:, 6, 0:4], 1.0 / D, RMS_EPS, ALU.mult, ALU.add))
                rsqrt(own, VAR, Y, A)

                def diag(q, col):
                    own(v.tensor_tensor(DG[:, q, :].rearrange("p (j n) -> p j n", n=P), ident[:, None, :].to_broadcast([P, TT, P]),
                                        col[:, :, None].to_broadcast([P, TT, P]), ALU.mult), "diag_ready", wait=False)

                diag(0, Y)
                if ln:
                    own(v.scalar_tensor_tensor(NB, MU, -1.0, Y, ALU.mult, ALU.mult))
                    diag(1, NB)
                dve.wait_ge(S["bcast_ready"], e["dg_at"] + 1)

                def normed(k):
                    if ln:
                        own(v.tensor_tensor(XT[:, k % 2, :], R[:, k, :], ps[:, 7, :], ALU.mult))
                        if k == 0:
                            dve.wait_ge(S["bcast_ready"], e["dg_at"] + 2)
                        own(v.tensor_tensor(XT[:, k % 2, :], XT[:, k % 2, :], ps[:, 6, :], ALU.add), "t_ready")
                    else:
                        own(v.tensor_tensor(XT[:, k % 2, :], R[:, k, :], ps[:, 7, :], ALU.mult), "t_ready")

                normed(0)
                for k in range(KD):
                    if k + 1 < KD:
                        normed(k + 1)
                    dve.wait_ge(S["xh_ready"], 8 * e["c"] + k + 1)
                    if ln or e["keep"]:
                        own(v.tensor_tensor(XL[:, k, :], R[:, k, :], XH[:, k, :].bitcast(F32), ALU.subtract), "x_ready")
                    else:
                        own(v.scalar_tensor_tensor(XL[:, k, :], XT[:, k % 2, :], vcol(e["gain"][0], e["gain"][1] * 8 + k),
                                                   XH[:, k, :].bitcast(F32), ALU.mult, ALU.subtract), "x_ready")
                own(v.memset(S1[:], 0.0))
                own(v.memset(S2[:], 0.0))

            stages = dict(load=load, ffn=ffn, norm=norm,
                          **{k: (lambda m: lambda e: m["dve"](dve, own, e, residual))(m) for k, m in mixers.items()})
            for e in st:
                if e["kind"] in stages:
                    stages[e["kind"]](e)


def rsqrt(own, x, y, a):
    v = own.eng
    own(v.tensor_scalar(a.bitcast(I32), x.bitcast(I32), 1, None, ALU.arith_shift_right))
    own(v.tensor_scalar(y.bitcast(I32), a.bitcast(I32), -1.0, float(0x5F3759DF), ALU.mult, ALU.add))
    own(v.tensor_scalar(x, x, -0.5, None, ALU.mult))
    for _ in range(3):
        own(v.tensor_tensor(a, y, y, ALU.mult))
        own(v.tensor_tensor(a, a, x, ALU.mult))
        own(v.scalar_tensor_tensor(y, a, 1.5, y, ALU.add, ALU.mult))


def outproj_pe(pe, b, e, n0, ready, xh, xl):
    S, ps = b["S"], b["ps"]
    for u in range(4):
        if u >= 2:
            pe.wait_ge(S["r_ready"], 8 * e["p"] + 2 * u)
        bank = 4 + 2 * (u % 2)
        b["fm_unit"](pe, n0 + u, (n0 + u) % 2, [(ps[:, bank, :], 0), (ps[:, bank + 1, :], P)], xh, xl, range(8), 256,
                     wait_k=ready)


def outproj_dve(b, e, n0, residual):
    for k in range(KD):
        residual(e, 0, k, 8, 4 + k % 4, b["unit_done_at"](n0 + k // 2))


CAUSAL = {3: (0, 0, 4), 0: (512, 0, 1), 2: (640, 0, 3), 1: (1024, 0, 2)}
BANDED = {1: (0, 0, 3), 2: (512, 1, 3), 0: (1024, 0, 2), 3: (1280, 2, 2)}


def flat(ps, bank):
    return ps[:, bank:bank + 3, :].rearrange("p a n -> p (a n)")


def reduce_angle(nc, own, A, K, KH, sin_of, cos_of):
    v = nc.vector
    import numpy as np
    two_pi = 2 * np.pi
    pieces, rest = [], two_pi
    for bits in (9, 21, 33):
        c = np.floor(rest * 2.0 ** bits) / 2.0 ** bits
        pieces.append(float(c))
        rest -= c
    pieces.append(float(np.float32(rest)))
    MAGIC = float(1.5 * 2 ** 23)
    BIG = float(1.5 * 2 ** 35)
    own(v.tensor_scalar(K, A, float(1 / two_pi), MAGIC, ALU.mult, ALU.add))
    own(v.tensor_scalar(K, K, MAGIC, None, ALU.subtract))
    own(v.tensor_scalar(KH, K, BIG, None, ALU.add))
    own(v.tensor_scalar(KH, KH, BIG, None, ALU.subtract))
    own(v.tensor_tensor(K, K, KH, ALU.subtract))
    for c in pieces:
        for k in (KH, K):
            own(v.scalar_tensor_tensor(A, k, -c, A, ALU.mult, ALU.add))
    top = 3.1415925
    own(v.tensor_scalar(sin_of, A, top, -top, ALU.min, ALU.max), "angle_ready")
    own(v.tensor_scalar(K, A, float(np.pi / 2), None, ALU.add))
    own(v.tensor_scalar(KH, K, float(np.pi), -two_pi, ALU.is_gt, ALU.mult))
    own(v.tensor_tensor(K, K, KH, ALU.add))
    own(v.tensor_scalar(cos_of, K, top, -top, ALU.min, ALU.max), "angle_ready")


def rope_angles(nc, own, PI, PF, W, freq):
    own(nc.vector.tensor_copy(PF, PI))
    own(nc.vector.tensor_scalar(W[0], PF, freq, None, ALU.mult))
    reduce_angle(nc, own, W[0], W[1], W[2], W[3], W[0])


def ev_attn(nc, b):
    S, ps, sb, sem, WORK, WORK2 = (b[k] for k in ("S", "ps", "sb", "sem", "WORK", "WORK2"))
    ident, ones, io, vcol, done_at, XHk, XLk = (b[k] for k in ("ident", "ones", "io", "vcol", "unit_done_at", "XHk", "XLk"))
    XH, XL, WH, WL = (b[k] for k in ("XH", "XL", "WH", "WL"))
    KB = 1024
    NH = 8
    LAM0 = 0.2
    SCALE = 64 ** -0.5
    Q = sb("da_q", [P, NH, T], at=WORK)
    K = sb("da_k", [P, NH, T], at=WORK + 16 * KB)
    V = sb("da_v", [P, TT, D], at=WORK + 32 * KB)
    O = sb("da_o", [P, NH, T], at=WORK + 48 * KB)
    YH = sb("da_yh", [P, NH, T], F32R, at=WORK)
    YL = sb("da_yl", [P, NH, T], F32R, at=WORK + 16 * KB)
    PR = sb("da_p", [P, 4, 1280], at=WORK + 64 * KB)
    COS = sb("da_cos", [P, T], at=WORK + 64 * KB)
    SIN = sb("da_sin", [P, T], at=WORK + 66 * KB)
    LB = sb("da_lb", [P, 4, 64], at=WORK + 68 * KB)
    LP = sb("da_lp", [P, 2, 64], at=WORK + 69 * KB)
    PI = sb("da_pi", [P, T], I32, at=WORK + 70 * KB)
    PF = sb("da_pf", [P, T], at=WORK + 72 * KB)
    C0 = WORK + 84 * KB
    perm = sb("da_perm", [P, P], at=C0)
    cmask = sb("da_mask", [P, P], at=C0 + 512)
    sm = sb("da_small", [P, 256], at=C0 + 1024)
    freq = sb("da_freq", [P, 2], at=C0 + 2048)
    GAIN = sb("da_gain", [P, 1], at=C0 + 2080)
    ANG = [sb(f"da_ang{i}", [P, T], at=WORK + (48 + 2 * i) * KB) for i in range(4)]
    QS = sb("da_qs", [P, 4, T], at=WORK2 + 8 * KB)
    AB = sb("da_ab", [P, 2, T], at=WORK2 + 16 * KB)
    PT = sb("da_pt", [P, 1280], at=WORK2 + 8 * KB)
    OSQ = sb("da_osq", [P, T], at=WORK2 + 14 * KB)
    YT = sb("da_yt", [P, 2, T], at=WORK2 + 16 * KB)
    DGA = sb("da_dg", [P, 2, T], at=WORK2 + 4 * KB)
    s = {n: sem("da_" + n) for n in """in v_ready qs_ready rot_ready rope_done angle_ready trig_ready lam_e lam_in
         scores max_ready p_ready comb tr pt_ready o_ready o_taken osq ssq dg bc bc_taken yh yl""".split()}
    order = [3, 0, 2, 1]
    MX, NM, L, RC, N2 = sm[:, 0:8], sm[:, 8:24], sm[:, 24:40], sm[:, 40:48], sm[:, 48:52]
    LAMS, LAM = sm[:, 52:54], sm[:, 54:55]
    SS, RS, TMPA = sm[:, 64:96], sm[:, 96:128], sm[:, 128:160]
    PTO = {0: 0, 1: 512, 3: 896, 2: 1024}

    def pe(pe, e):
        mm, three = b["mm"], b["pe_three"]
        for h in range(2):
            for g in range(2):
                n = e["nv"] + 2 * h + g
                pe.wait_ge(S["split_ready"], n + 1)
                for q in range(4):
                    k = 4 * g + q
                    if h == 0:
                        pe.wait_ge(S["x_ready"], 8 * e["x"] + k + 1)
                    for j in range(TT):
                        ws = slice(512 * q, 512 * q + 512)
                        ts = slice(P * j, P * j + P)
                        mm(ps[:, 4 * h + j, :], XH[:, k, ts], WH[:, n % 2, ws], k == 0, False)
                        mm(ps[:, 4 * h + j, :], XL[:, k, ts], WH[:, n % 2, ws], False, False)
                        last = mm(ps[:, 4 * h + j, :], XH[:, k, ts], WL[:, n % 2, ws], False, k == 7)
                last.then_inc(S["unit_done"], 1)

        def rot(u):
            pe.wait_ge(s["qs_ready"], 2 * u + 2)
            pe.wait_ge(s["in"], 64)
            if u >= 2:
                pe.wait_ge(s["rope_done"], 2 * u - 2)
            for t in range(2):
                mm(ps[:, 4 + 2 * (u % 2) + t, :], perm[:], QS[:, 2 * (u % 2) + t, :]).then_inc(s["rot_ready"], 1)

        for u in range(8):
            pe.wait_ge(s["v_ready"], 4 if u < 2 else 8)
            if u >= 2:
                pe.wait_ge(s["qs_ready"], 2 * u - 2)
            bank = 2 * (u % 2)
            b["fm_unit"](pe, e["nq"] + u, (e["nq"] + u) % 2, [(ps[:, bank, :], 0), (ps[:, bank + 1, :], P)], XHk, XLk, range(8), 256)
            if u:
                if u == 1:
                    pe.wait_ge(s["v_ready"], 8)
                rot(u - 1)
        rot(7)

        def scores(h):
            for c in range(2):
                if h:
                    pe.wait_ge(s["p_ready"], 8 * (h - 1) + 4 * c + 4)
                else:
                    pe.wait_ge(s["rope_done"], 16)
                fl, rows = flat(ps, 3 * c), slice(64 * c, 64 * c + 64)
                for i in order:
                    o, k0, nk = CAUSAL[i]
                    mm(fl[:, o:o + nk * P], Q[rows, h, i * P:(i + 1) * P], K[rows, h, 0:nk * P], True, False)
                    last = mm(fl[:, o + i * P:o + nk * P], ident[:], cmask[:], False, True)
                last.then_inc(s["scores"], 1)

        scores(0)
        for h in range(NH):
            if h + 1 < NH:
                scores(h + 1)
            pe.wait_ge(s["comb"], 4 * h + 4)
            for j in range(TT):
                if j >= 2:
                    pe.wait_ge(s["pt_ready"], 4 * h + j - 1)
                elif h:
                    pe.wait_ge(s["o_taken"], 2 * h)
                    pe.wait_ge(s["pt_ready"], 4 * h)
                for i in range(j, TT):
                    o, _, _ = CAUSAL[i]
                    last = nc.tensor.transpose(ps[:, 6 + j % 2, (i - j) * P:(i - j + 1) * P],
                                               PR[:, 2 * (h % 2), o + j * P:o + (j + 1) * P], ident[:])
                last.then_inc(s["tr"], 1)
            pe.wait_ge(s["pt_ready"], 4 * h + 4)
            for j in range(TT):
                last = mm(ps[:, 6, j * P:512], V[:, j, h * P:(h + 1) * P], PT[:, PTO[j]:PTO[j] + (4 - j) * P], j == 0, j == 3)
            last.then_inc(s["o_ready"], 1)
            pe.wait_ge(s["osq"], h + 1)
            for j in range(TT):
                last = mm(ps[:, 5, 480 + 4 * h + j:481 + 4 * h + j], OSQ[:, j * P:(j + 1) * P], ones[:, 0:1])
            last.then_inc(s["ssq"], 1)
        for h in range(NH):
            pe.wait_ge(s["dg"], h + 1)
            if h >= 2:
                pe.wait_ge(s["bc_taken"], h - 1)
            mm(ps[:, h % 2, :], ones[:], DGA[:, h % 2, :]).then_inc(s["bc"], 1)
        outproj_pe(pe, b, e, e["no"], lambda k: pe.wait_ge(s["yl"], k + 1), lambda k: YH[:, k, :], lambda k: YL[:, k, :])

    def act(act, own, e):
        c0 = CONSTS
        act.wait_ge(S["x_ready"], 8 * e["x"] + 8)
        act.dma_start(LB[:].rearrange("p a n -> p (a n)"), io["ev_lambdas"].rearrange("a b c -> a (b c)").to_broadcast([P, 256])).then_inc(s["lam_in"], 16)
        act.dma_start(PI[:], io["positions"].to_broadcast([P, T])).then_inc(s["in"], 16)
        for dst, name in ((perm, "perm64"), (cmask, "chunk"), (freq, "freq")):
            a, n = c0[name]
            act.dma_start(dst[:], io["constants"][:, a:a + n]).then_inc(s["in"], 16)
        own2 = b["Own"](act, {"trig_ready": s["trig_ready"]}, "trig_ready")
        act.wait_ge(s["angle_ready"], 1)
        own2(nc.scalar.activation(SIN[:], ANG[3][:], ACT.Sin))
        act.wait_ge(s["angle_ready"], 2)
        own2(nc.scalar.activation(COS[:], ANG[0][:], ACT.Sin))
        act.wait_ge(s["lam_e"], 1)
        nc.scalar.activation(LAMS, LAMS, ACT.Exp).then_inc(s["lam_e"], 1)
        for h in range(2):
            act.wait_ge(S["unit_done"], done_at(e["nv"] + 2 * h + 1))
            for j in range(TT):
                nc.scalar.activation(V[:, j, 512 * h:512 * h + 512], ps[:, 4 * h + j, :], ACT.Copy).then_inc(s["v_ready"], 1)
        for u in range(8):
            act.wait_ge(S["unit_done"], done_at(e["nq"] + u))
            if u >= 2:
                act.wait_ge(s["rope_done"], 2 * u - 2)
            for t in range(2):
                nc.scalar.activation(QS[:, 2 * (u % 2) + t, :], ps[:, 2 * (u % 2) + t, :], ACT.Copy).then_inc(s["qs_ready"], 1)

        def exps(h):
            for c in range(2):
                act.wait_ge(s["max_ready"], 2 * h + c + 1)
                if h >= 2:
                    act.wait_ge(s["tr"], 4 * (h - 1))
                for q, i in enumerate(order):
                    o, _, nk = CAUSAL[i]
                    z = 8 * (h % 2) + 4 * c + q
                    nc.scalar.activation(PR[:, 2 * (h % 2) + c, o:o + nk * P], flat(ps, 3 * c)[:, o:o + nk * P], ACT.Exp,
                                         scale=SCALE, bias=NM[:, z:z + 1], accum_out=L[:, z:z + 1])\
                        .then_inc(s["p_ready"], 1)

        exps(0)
        for h in range(NH):
            for j in range(TT):
                act.wait_ge(s["tr"], 4 * h + j + 1)
                nc.scalar.activation(PT[:, PTO[j]:PTO[j] + (4 - j) * P], ps[:, 6 + j % 2, 0:(4 - j) * P], ACT.Copy)\
                    .then_inc(s["pt_ready"], 1)
            if h + 1 < NH:
                exps(h + 1)
            act.wait_ge(s["o_taken"], 2 * h + 1)
            if h:
                act.wait_ge(s["ssq"], h)
            nc.scalar.activation(OSQ[:], O[:, h, :], ACT.Square).then_inc(s["osq"], 1)
        for h in range(NH):
            act.wait_ge(s["bc_taken"], h + 1)
            nc.scalar.activation(YH[:, h, :], YT[:, h % 2, :], ACT.Copy).then_inc(s["yh"], 1)

    def dve(dve, own, e, residual):
        v = nc.vector
        own.knows(s)
        dve.wait_ge(S["x_ready"], 8 * e["x"] + 8)
        dve.wait_ge(s["in"], 64)
        rope_angles(nc, own, PI[:], PF[:], [a[:] for a in ANG], freq[:, 0:1])
        dve.wait_ge(s["lam_in"], 16)
        own(v.tensor_tensor(LP[:], LB[:].rearrange("p (a c) n -> p a c n", c=2)[:, :, 0, :],
                            LB[:].rearrange("p (a c) n -> p a c n", c=2)[:, :, 1, :], ALU.mult))
        own(v.tensor_reduce(LAMS, LP[:], AX.X, ALU.add), "lam_e")
        dve.wait_ge(s["lam_e"], 2)
        own(v.tensor_tensor(LAM, LAMS[:, 1:2], LAMS[:, 0:1], ALU.subtract))
        own(v.tensor_scalar(LAM, LAM, -LAM0, None, ALU.add))
        own(v.tensor_scalar(GAIN[:], vcol("subln", 0), 1.0 - LAM0, None, ALU.mult))
        dve.wait_ge(s["trig_ready"], 2)
        for u in range(8):
            for t in range(2):
                g = 2 * u + t
                dve.wait_ge(s["qs_ready"], g + 1)
                own(v.tensor_tensor(AB[:, 0, :], QS[:, 2 * (u % 2) + t, :], COS[:], ALU.mult), wait=False)
                dve.wait_ge(s["rot_ready"], g + 1)
                own(v.tensor_tensor(AB[:, 1, :], ps[:, 4 + 2 * (u % 2) + t, :], SIN[:], ALU.mult))
                dst = (Q if g < 8 else K)[:, g % 8, :]
                own(v.tensor_tensor(dst, AB[:, 0, :], AB[:, 1, :], ALU.add), "rope_done")

        def maxes(h):
            for c in range(2):
                dve.wait_ge(s["scores"], 2 * h + c + 1)
                for q, i in enumerate(order):
                    o, _, nk = CAUSAL[i]
                    own(v.tensor_reduce(MX[:, 4 * c + q:4 * c + q + 1], flat(ps, 3 * c)[:, o:o + nk * P], AX.X, ALU.max),
                        wait=q == 3)
                z = 8 * (h % 2) + 4 * c
                own(v.tensor_scalar(NM[:, z:z + 4], MX[:, 4 * c:4 * c + 4], -SCALE, None, ALU.mult), "max_ready")

        maxes(0)
        for h in range(NH):
            dve.wait_ge(s["p_ready"], 8 * h + 8)
            z = 8 * (h % 2)
            own(v.reciprocal(RC, L[:, z:z + 8]))
            own(v.tensor_scalar(N2, RC[:, 4:8], LAM, None, ALU.mult))
            for q, i in enumerate(order):
                o, _, nk = CAUSAL[i]
                p2 = PR[:, 2 * (h % 2) + 1, o:o + nk * P]
                own(v.tensor_scalar(p2, p2, N2[:, q:q + 1], None, ALU.mult), wait=q == 3)
            for q, i in enumerate(order):
                o, _, nk = CAUSAL[i]
                p1, p2 = (PR[:, 2 * (h % 2) + c, o:o + nk * P] for c in range(2))
                own(v.scalar_tensor_tensor(p1, p1, RC[:, q:q + 1], p2, ALU.mult, ALU.add), "comb", wait=q == 3)
            if h + 1 < NH:
                maxes(h + 1)
            dve.wait_ge(s["o_ready"], h + 1)
            own(v.tensor_copy(O[:, h, :], ps[:, 6, :]), "o_taken")
            dve.sem_inc(s["o_taken"], 1)
            own.n["o_taken"] += 1
        dve.wait_ge(s["ssq"], NH)
        own(v.tensor_scalar(SS, ps[:, 5, 480:512], 1.0 / P, RMS_EPS, ALU.mult, ALU.add))
        rsqrt(own, SS, RS, TMPA)

        def dg(h):
            own(v.tensor_tensor(DGA[:, h % 2, :].rearrange("p (j n) -> p j n", n=P), ident[:, None, :].to_broadcast([P, TT, P]),
                                RS[:, 4 * h:4 * h + 4][:, :, None].to_broadcast([P, TT, P]), ALU.mult), "dg")

        dg(0)
        for h in range(NH):
            if h + 1 < NH:
                dg(h + 1)
            dve.wait_ge(s["bc"], h + 1)
            own(v.scalar_tensor_tensor(YT[:, h % 2, :], O[:, h, :], GAIN[:], ps[:, h % 2, :], ALU.mult, ALU.mult), "bc_taken")
            dve.wait_ge(s["yh"], h + 1)
            own(v.tensor_tensor(YL[:, h, :], YT[:, h % 2, :], YH[:, h, :].bitcast(F32), ALU.subtract), "yl")
        outproj_dve(b, e, e["no"], residual)

    return dict(pe=pe, act=act, dve=dve)




ROWCOL = {0: 0, 1: 512, 3: 896, 2: 1024}


def ev_mamba(nc, b):
    S, ps, sb, sem, WORK, WORK2 = (b[k] for k in ("S", "ps", "sb", "sem", "WORK", "WORK2"))
    ident, ones, io, vcol, done_at, XHk, XLk = (b[k] for k in ("ident", "ones", "io", "vcol", "unit_done_at", "XHk", "XLk"))
    XH, XL, S2, SQ = (b[k] for k in ("XH", "XL", "S2", "SQ"))
    KB = 1024
    NH, HD = 16, 64
    XS = sb("mb_xs", [P, 8, T], at=WORK)
    BC = sb("mb_bc", [P, 4, T], at=WORK + 16 * KB)
    ZS = sb("mb_zs", [P, 8, T], at=WORK + 24 * KB)
    XDT = sb("mb_xdt", [P, TT, D], at=WORK + 40 * KB)
    CB = sb("mb_cb", [P, 2, 1280], at=WORK + 56 * KB)
    E = sb("mb_e", [P, 2, 1280], at=WORK + 66 * KB)
    AR = sb("mb_rows", [16, 1280], at=WORK + 76 * KB)
    tri = sb("mb_tri", [P, P], at=WORK + 81 * KB)
    le = sb("mb_le", [P, P], at=WORK + 81 * KB + 512)
    gt = sb("mb_gt", [P, P], at=WORK + 82 * KB)
    half = sb("mb_half", [2, P], at=WORK + 82 * KB + 512)
    d2 = sb("mb_d2", [2, 8], at=WORK + 83 * KB)
    bias = sb("mb_bias", [P, 2, 16], at=WORK + 83 * KB + 64)
    tm = sb("mb_tm", [P, 10, 64], at=WORK + 83 * KB + 256)
    cw = sb("mb_cw", [P, 60], at=WORK + 86 * KB)
    dskip = sb("mb_dskip", [P, 8], at=WORK + 86 * KB + 256)
    DTR = sb("mb_dtr", [16, T], at=WORK2 + 4 * KB)
    CV = sb("mb_cv", [P, 2, T], at=WORK2 + 8 * KB)
    TA = sb("mb_ta", [P, 2, T], at=WORK2 + 12 * KB)
    YT = sb("mb_yt", [P, 2, T], at=WORK2 + 16 * KB)
    DG = sb("mb_dg", [P, T], at=WORK2 + 12 * KB)
    DT, DA, U0, U1, U2, U3, NLOC, SUF, EE, RS = (tm[:, i, :] for i in range(10))
    s = {n: sem("mb_" + n) for n in """in dt_ev dt_t dt_x dt_e dt_done rows rows_ev small conv tanh xs_done z_tanh z_done
         xt xdt cb cb_ev bcast exp m y y_taken y_ready sq gs dg bc g1 yh""".split()}
    v3 = lambda a: a.rearrange("p (j h) -> p j h", h=16)

    def pe(pe, e):
        mm = b["mm"]
        pe.wait_ge(S["x_ready"], 8 * e["x"] + 8)
        pe.wait_ge(S["r_ready"], 8 * e["p"] + 2)
        b["fm_unit"](pe, e["nd"], e["nd"] % 2, [(ps[:, 7, :], 0)], XHk, XLk, range(8), P)
        for u in range(6):
            if u >= 2:
                pe.wait_ge(s["xs_done"], 2 * u - 2)
            bank = 2 * (u % 2)
            b["fm_unit"](pe, e["nx"] + u, (e["nx"] + u) % 2, [(ps[:, bank, :], 0), (ps[:, bank + 1, :], P)], XHk, XLk, range(8), 256)
            if u == 0:
                pe.wait_ge(s["dt_ev"], 1)
                for j in range(TT):
                    last = nc.tensor.transpose(ps[:, 6, 16 * j:16 * j + 16], DTR[:, j * P:(j + 1) * P], ident[0:16, 0:16])
                last.then_inc(s["dt_t"], 1)
            if u == 1:
                pe.wait_ge(s["in"], 128)
                pe.wait_ge(s["dt_done"], 1)
                mm(ps[:, 6, 64:72], half[:], d2[:])
                mm(ps[:, 6, 128:192], le[:], DA)
                mm(ps[:, 6, 192:256], gt[:], DA).then_inc(s["small"], 1)
                pe.wait_ge(s["dt_ev"], 1)
                for i in range(TT):
                    for q, j in enumerate(range(i, TT)):
                        bank, col = {0: (4, 0), 1: (5, 0), 2: (7, 0), 3: (5, 384)}[i]
                        out = ps[0:16, bank, col + q * P:col + (q + 1) * P]
                        between = list(range(i + 1, j))
                        last = mm(out, DA[:, 16 * j:16 * j + 16], le[:], True, not between)
                        for m in between:
                            last = mm(out, DA[:, 16 * m:16 * m + 16], ones[:], False, m == between[-1])
                last.then_inc(s["rows"], 1)
        for u in range(4):
            bank = 2 * (u % 2)
            pe.wait_ge(s["xs_done"], min(8 + 2 * u + 2, 12)) if u < 2 else pe.wait_ge(s["z_done"], 2 * u - 2)
            b["fm_unit"](pe, e["nz"] + u, (e["nz"] + u) % 2, [(ps[:, bank, :], 0), (ps[:, bank + 1, :], P)], XHk, XLk, range(8), 256)
            if u == 0:
                pe.wait_ge(s["rows_ev"], 3)
                pe.wait_ge(s["xs_done"], 12)
            for q in (2 * u, 2 * u + 1):
                j, h = q // 2, q % 2
                if q >= 2:
                    pe.wait_ge(s["xdt"], q - 1)
                for c in range(4):
                    last = nc.tensor.transpose(ps[:, 4 + q % 2, c * P:(c + 1) * P], XS[:, 4 * h + c, j * P:(j + 1) * P], ident[:])
                last.then_inc(s["xt"], 1)
        pe.wait_ge(s["z_done"], 8)
        pe.wait_ge(s["xdt"], 8)
        for g in range(2):
            for i in range(TT):
                o = ROWCOL[i]
                last = mm(flat(ps, 3 * g)[:, o:o + (4 - i) * P], BC[:, g, i * P:(i + 1) * P], BC[:, 2 + g, i * P:T])
            last.then_inc(s["cb"], 1)

        def spread(h):
            fl = flat(ps, 3 * (h % 2))
            pe.wait_ge(s["exp"], 7 * (h - 1)) if h >= 2 else pe.wait_ge(s["cb_ev"], 6)
            one = ident[0:16, h:h + 1].to_broadcast([16, P])
            for a, n in ((0, 512), (512, 512), (1024, 256)):
                mm(fl[:, a:a + n], one, AR[:, a:a + n], True, False)
                tiles = [o for o in ROWCOL.values() if a <= o < a + n]
                for o in tiles:
                    last = mm(fl[:, o:o + P], ident[:], tri[:], False, o == tiles[-1])
            last.then_inc(s["bcast"], 1)

        spread(0)
        for h in range(NH):
            if h + 1 < NH:
                spread(h + 1)
            c = h // 2
            if h % 2 == 0 and c >= 2:
                pe.wait_ge(s["y_taken"], c - 1)
            pe.wait_ge(s["m"], h + 1)
            out = ps[64 * (h % 2):64 * (h % 2) + 64, 6 + c % 2, :]
            for i in range(TT):
                o = ROWCOL[i]
                last = mm(out[:, i * P:T], XDT[:, i, h * HD:(h + 1) * HD], E[:, h % 2, o:o + (4 - i) * P], i == 0, i == 3)
            last.then_inc(s["y"], 1)
        pe.wait_ge(s["gs"], 8)
        for j in range(TT):
            last = mm(ps[:, 0, j:j + 1], S2[:, j * P:(j + 1) * P], ones[:, 0:1])
        last.then_inc(s["dt_t"], 1)
        pe.wait_ge(s["dg"], 1)
        mm(ps[:, 1, :], ones[:], DG[:]).then_inc(s["bc"], 1)
        outproj_pe(pe, b, e, e["no"], lambda k: pe.wait_ge(S["x_ready"], 8 * (e["x"] + 1) + k + 1), XHk, XLk)

    def act(act, own, e):
        own.knows(s)
        A = nc.scalar.activation
        act.wait_ge(S["r_ready"], 8 * e["p"] + 2)
        for dst, name, r in ((tri, "tri", P), (le, "le", P), (gt, "gt", P), (half, "half", 2)):
            a, n = CONSTS[name]
            act.dma_start(dst[:], io["constants"][0:r, a:a + n]).then_inc(s["in"], 16)
        act.dma_start(bias[:, 0, :], io["ev_dt_bias"].to_broadcast([P, 16])).then_inc(s["in"], 16)
        act.dma_start(bias[:, 1, :], io["ev_a_log"].to_broadcast([P, 16])).then_inc(s["in"], 16)
        for r in range(2):
            with nc.allow_non_contiguous_dma(reason="16 numbers"):
                act.dma_start(d2[r:r + 1, :], io["ev_d_skip"].rearrange("a (c h) -> a h c", h=2)[:, r, :]).then_inc(s["in"], 16)
        act.wait_ge(S["unit_done"], done_at(e["nd"]))
        A(DTR[:], ps[0:16, 7, :], ACT.Copy).then_inc(s["dt_ev"], 1)
        act.wait_ge(s["in"], 128)
        own(A(bias[:, 1, :], bias[:, 1, :], ACT.Exp), "dt_e")
        act.wait_ge(s["dt_x"], 1)
        own(A(EE, EE, ACT.Exp, scale=-1.0), "dt_e")

        def conv_tanh(g):
            act.wait_ge(s["conv"], g + 1)
            A(TA[:, g % 2, :], CV[:, g % 2, :], ACT.Tanh).then_inc(s["tanh"], 1)

        for g in range(12):
            conv_tanh(g)
            if g == 5:
                act.wait_ge(s["rows"], 1)
                for bank, col, n in ((4, 0, 512), (5, 512, 512), (7, 1024, 256)):
                    A(AR[:, col:col + n], ps[0:16, bank, 0:n], ACT.Copy).then_inc(s["rows_ev"], 1)
        for g in range(8):
            act.wait_ge(S["unit_done"], done_at(e["nz"] + g // 2))
            act.wait_ge(s["z_done"], g - 1) if g >= 2 else act.wait_ge(s["xs_done"], 12)
            A(TA[:, g % 2, :], ps[:, 2 * (g // 2 % 2) + g % 2, :], ACT.Tanh, scale=0.5).then_inc(s["z_tanh"], 1)
        for g in range(2):
            act.wait_ge(s["cb"], g + 1)
            for q in range(3):
                n = (512, 512, 256)[q]
                A(CB[:, g, 512 * q:512 * q + n], ps[:, 3 * g + q, 0:n], ACT.Copy).then_inc(s["cb_ev"], 1)
        for h in range(NH):
            act.wait_ge(s["bcast"], h + 1)
            if h >= 2:
                act.wait_ge(s["y"], h - 1)
            fl = flat(ps, 3 * (h % 2))
            for i in range(TT):
                o = ROWCOL[i]
                A(E[:, h % 2, o:o + P], fl[:, o:o + P], ACT.Exp, bias=v3(NLOC)[:, i, h:h + 1]).then_inc(s["exp"], 1)
                if i < 3:
                    A(E[:, h % 2, o + P:o + (4 - i) * P], fl[:, o + P:o + (4 - i) * P], ACT.Exp, bias=v3(SUF)[:, i, h:h + 1])\
                        .then_inc(s["exp"], 1)
            if h % 2:
                c = h // 2
                act.wait_ge(s["y_ready"], c + 1)
                if c >= 2:
                    act.wait_ge(s["gs"], c - 1)
                A(SQ[:, c % 2, :], ZS[:, c, :], ACT.Square).then_inc(s["sq"], 1)
        for k in range(8):
            act.wait_ge(s["g1"], k + 1)
            A(XH[:, k, :], YT[:, k % 2, :], ACT.Copy).then_inc(s["yh"], 1)
        b["square_act"](act, e)

    def dve(dve, own, e, residual):
        v = nc.vector
        own.knows(s)
        own(v.tensor_scalar(cw[:, 0:48], vcolN("conv_w", 48), 0.5, None, ALU.mult))
        own(v.tensor_scalar(cw[:, 48:60], vcolN("conv_b", 12), 0.5, None, ALU.mult))
        dve.wait_ge(s["in"], 128)
        dve.wait_ge(s["dt_t"], 1)
        bc = lambda q: bias[:, q:q + 1, :].to_broadcast([P, TT, 16])
        own(v.tensor_tensor(v3(U0), v3(ps[:, 6, 0:64]), bc(0), ALU.add))
        own(v.scalar_tensor_tensor(EE, U0, -1.0, U0, ALU.mult, ALU.max), "dt_x")
        dve.wait_ge(s["dt_e"], 2)
        own(v.tensor_scalar(U1, EE, 2.0, None, ALU.add))
        own(v.reciprocal(U1, U1))
        own(v.tensor_tensor(U1, U1, EE, ALU.mult))
        own(v.tensor_tensor(U2, U1, U1, ALU.mult))
        own(v.memset(U3, 1.0 / 19))
        for d in (17, 15, 13, 11, 9, 7, 5, 3, 1):
            own(v.tensor_tensor(U3, U3, U2, ALU.mult))
            own(v.tensor_scalar(U3, U3, 1.0 / d, None, ALU.add))
        own(v.scalar_tensor_tensor(U3, U3, 2.0, U1, ALU.mult, ALU.mult))
        own(v.scalar_tensor_tensor(DT, U0, 0.0, U3, ALU.max, ALU.add))
        own(v.scalar_tensor_tensor(v3(DA), v3(DT), -1.0, bc(1), ALU.mult, ALU.mult), "dt_done")

        def conv(g):
            c = TILES[g]
            x, y = ps[:, 2 * (g // 2 % 2) + g % 2, :], CV[:, g % 2, :]
            dve.wait_ge(S["unit_done"], done_at(e["nx"] + g // 2))
            if g >= 2:
                dve.wait_ge(s["tanh"], g - 1)
            own(v.tensor_scalar(y, x, cw[:, 36 + c:37 + c], cw[:, 48 + c:49 + c], ALU.mult, ALU.add))
            for d in (1, 2, 3):
                own(v.scalar_tensor_tensor(y[:, d:], x[:, 0:T - d], cw[:, 12 * (3 - d) + c:12 * (3 - d) + c + 1], y[:, d:],
                                           ALU.mult, ALU.add), "conv" if d == 3 else None)
            dve.wait_ge(s["tanh"], g + 1)
            dst = XS[:, c, :] if c < 8 else BC[:, c - 8, :]
            own(v.scalar_tensor_tensor(dst, TA[:, g % 2, :], 1.0, y, ALU.add, ALU.mult), "xs_done")

        TILES = [8, 9, 10, 11, 0, 1, 2, 3, 4, 5, 6, 7]
        for g in range(12):
            conv(g)
            if g == 4:
                dve.wait_ge(s["small"], 1)
                own(v.tensor_scalar(NLOC, ps[:, 6, 128:192], -1.0, None, ALU.mult))
                own(v.tensor_copy(SUF, ps[:, 6, 192:256]))
                own(v.tensor_copy(dskip[:], ps[:, 6, 64:72]))

        def xdt(q):
            j, h = q // 2, q % 2
            dve.wait_ge(s["xt"], q + 1)
            own(v.tensor_tensor(XDT[:, j, 512 * h:512 * h + 512].rearrange("p (h n) -> p h n", n=HD),
                                ps[:, 4 + q % 2, :].rearrange("p (h n) -> p h n", n=HD),
                                v3(DT)[:, j, 8 * h:8 * h + 8][:, :, None].to_broadcast([P, 8, HD]), ALU.mult), "xdt")

        for g in range(8):
            dve.wait_ge(s["z_tanh"], g + 1)
            own(v.scalar_tensor_tensor(ZS[:, g, :], TA[:, g % 2, :], 1.0, ps[:, 2 * (g // 2 % 2) + g % 2, :], ALU.add, ALU.mult), "z_done")
            if g % 2:
                xdt(g - 1)
                xdt(g)
        for h in range(NH):
            if h == 0:
                dve.wait_ge(s["cb_ev"], 6)
            dve.wait_ge(s["exp"], 7 * h + 7)
            own(v.tensor_tensor(E[:, h % 2, :], E[:, h % 2, :], CB[:, h // 8, :], ALU.mult), "m")
            if h % 2:
                c = h // 2
                dve.wait_ge(s["y"], h + 1)
                own(v.scalar_tensor_tensor(YT[:, 0, :], XS[:, c, :], dskip[:, c:c + 1], ps[:, 6 + c % 2, :], ALU.mult, ALU.add), "y_taken")
                own(v.scalar_tensor_tensor(ZS[:, c, :], YT[:, 0, :], 0.5, ZS[:, c, :], ALU.mult, ALU.mult), "y_ready")
                if c:
                    dve.wait_ge(s["sq"], c)
                    own(v.tensor_tensor(S2[:], S2[:], SQ[:, (c - 1) % 2, :], ALU.add), "gs")
        dve.wait_ge(s["sq"], 8)
        own(v.tensor_tensor(S2[:], S2[:], SQ[:, 1, :], ALU.add), "gs")
        dve.wait_ge(s["dt_t"], 2)
        own(v.tensor_scalar(U0[:, 0:4], ps[:, 0, 0:4], 1.0 / D, RMS_EPS, ALU.mult, ALU.add))
        rsqrt(own, U0[:, 0:4], RS[:, 0:4], U1[:, 0:4])
        own(v.tensor_tensor(DG[:].rearrange("p (j n) -> p j n", n=P), ident[:, None, :].to_broadcast([P, TT, P]),
                            RS[:, 0:4][:, :, None].to_broadcast([P, TT, P]), ALU.mult), "dg")
        own(v.memset(S2[:], 0.0))
        dve.wait_ge(s["bc"], 1)

        def g1(k):
            own(v.scalar_tensor_tensor(YT[:, k % 2, :], ZS[:, k, :], vcol("gate_norm", k), ps[:, 1, :], ALU.mult, ALU.mult), "g1")

        g1(0)
        for k in range(8):
            if k + 1 < 8:
                g1(k + 1)
            dve.wait_ge(s["yh"], k + 1)
            own(v.tensor_tensor(XL[:, k, :], YT[:, k % 2, :], XH[:, k, :].bitcast(F32), ALU.subtract), "x_ready")
        outproj_dve(b, e, e["no"], residual)

    def vcolN(name, n):
        c = b["vec_col"][name]
        return b["VEC"][:, c:c + n]

    return dict(pe=pe, act=act, dve=dve)





def od_mixer(nc, b):
    S, ps, sb, sem, WORK, WORK2 = (b[k] for k in ("S", "ps", "sb", "sem", "WORK", "WORK2"))
    ident, ones, io, vcol, done_at, XHk, XLk = (b[k] for k in ("ident", "ones", "io", "vcol", "unit_done_at", "XHk", "XLk"))
    XH, XL, WH, WL, SQ = (b[k] for k in ("XH", "XL", "WH", "WL", "SQ"))
    KB = 1024
    NH = 8
    SCALE = 96 ** -0.5
    r = slice(64, 96)
    U = sb("od_u", [P, 4, T], at=WORK)
    Q = sb("od_q", [P, NH, T], at=WORK + 8 * KB)
    K = sb("od_k", [P, NH, T], at=WORK + 24 * KB)
    V = sb("od_v", [P, TT, 512], at=WORK + 40 * KB)
    RAWC = sb("od_rawc", [P, 5, T], at=WORK + 24 * KB)
    SQC = sb("od_sqc", [P, 5, T], at=WORK + 34 * KB)
    KRS = sb("od_krs", [P, T], at=WORK + 44 * KB)
    KR = sb("od_kr", [P, T], at=WORK + 46 * KB)
    PR = sb("od_p", [P, 2, 1280], at=WORK + 48 * KB)
    CKH = sb("od_ckh", [P, 2, T], F32R, at=WORK + 48 * KB)
    CKL = sb("od_ckl", [P, 2, T], F32R, at=WORK + 52 * KB)
    TC = sb("od_tc", [P, 4, T], at=WORK + 58 * KB)
    TS = sb("od_ts", [P, 4, T], at=WORK + 66 * KB)
    CQH = sb("od_cqh", [P, 3, T], F32R, at=WORK + 74 * KB)
    CQL = sb("od_cql", [P, 3, T], F32R, at=WORK + 80 * KB)
    TC1 = sb("od_tc1", [P, 4, T], at=b["XH_AT"])
    TS1 = sb("od_ts1", [P, 4, T], at=b["XH_AT"] + 16 * KB)
    VR, VI, ZR, ZI, TA, TB = (sb(f"od_w{i}", [P, T], at=WORK + (74 + 2 * i) * KB) for i in range(6))
    GH = sb("od_gh", [P, 4, T], F32R, at=WORK + 58 * KB)
    GL = sb("od_gl", [P, 4, T], F32R, at=WORK + 66 * KB)
    PT = sb("od_pt", [P, 1280], at=WORK2 + 4 * KB)
    CN = sb("od_cn", [P, 2, T], at=WORK2 + 4 * KB)
    COS = sb("od_cos", [P, T], at=WORK2 + 8 * KB)
    SIN = sb("od_sin", [P, T], at=WORK2 + 10 * KB)
    AB = sb("od_ab", [P, 2, T], at=WORK2 + 16 * KB)
    BT = sb("od_bt", [P, 2, T], at=WORK2 + 12 * KB)
    CT = sb("od_ct", [P, 2, T], at=WORK2 + 16 * KB)
    YS = sb("od_ys", [P, T], at=WORK2 + 9 * KB + 256)
    ANG = [sb(f"od_ang{i}", [P, T], at=WORK + (58 + 2 * i) * KB) for i in range(4)]
    PI = sb("od_pi", [P, T], I32, at=WORK + 66 * KB)
    PF = sb("od_pf", [P, T], at=WORK + 68 * KB)
    LROW = sb("od_lrow", [16, 2, P], at=WORK + 70 * KB)
    half = sb("od_half", [2, P], at=WORK + 71 * KB)
    ls2 = sb("od_ls2", [2, 16], at=WORK + 71 * KB + 512)
    BIN = sb("od_bin", [P, 2, 16, 16], at=WORK2 + 16 * KB)
    BB = sb("od_bb", [P, 2, 16, 16], at=WORK + 72 * KB)
    BX = sb("od_bx", [P, 2, 16, 32], at=WORK + 66 * KB)
    CIN = sb("od_cin", [P, 2, 4, 64], at=WORK + 58 * KB)
    CX = sb("od_cx", [P, 2, 4, P], at=WORK + 60 * KB)
    DGC = sb("od_dg", [P, 2, T], at=WORK2 + 12 * KB)
    M0 = WORK + 86 * KB
    perm = sb("od_perm", [P, P], at=M0)
    cmask = sb("od_mask", [P, P], at=M0 + 512)
    small = sb("od_small", [P, 14, 16], at=M0 + 1024)
    SP = b["sb_small"]
    FREQ, PAR, BG = SP[:, 0:2], SP[:, 2:6], SP[:, 6:10]
    MX, NM, L, RC = SP[:, 10:14], SP[:, 14:22], SP[:, 22:30], SP[:, 30:34]
    SS, RS, TMPA = SP[:, 34:42], SP[:, 42:50], SP[:, 50:58]
    LR, LI, DE, ER, IM, XA, XK, XH_, XB, SN, CS, FR, FI, T0 = (small[:, i, :] for i in range(14))
    W2 = b["sb_w2"]
    SCR = {(late, m): sb(f"od_scr{m}{late}", [P, 4, m], at=WORK + 78 * KB if late else b["XH_AT"] + 12 * KB)
           for late in (False, True) for m in (1, 2, 4, 8, 16, 32, 64, 128, 256)}
    s = {n: sem("od_" + n) for n in """in c_in u_ev par_t angle_ready trig sq_ev stats dg bc cn hi cl q_ev rot rope_done
         k_mm k_ev exp_in params bt_t bt_done scores max_ready p_ready comb tr pt_ready o_ready o_hi bu bu_taken x yc
         y th gh gl table""".split()}
    order = [3, 0, 2, 1]
    PTO = {0: 0, 1: 512, 3: 896, 2: 1024}
    QB = [0, 1, 2, 5, 6, 7, 3, 4]

    def pe(pe, e):
        mm, three, unit = b["mm"], b["pe_three"], b["fm_unit"]
        nu = e["nu"]
        un = lambda i, outs, **kw: unit(pe, nu + i, (nu + i) % 2, outs, XHk, XLk, range(8), kw.pop("w", 256), **kw)
        un(0, [(ps[:, 0, :], 0), (ps[:, 1, :], P)], x_at=8 * e["x"])
        un(1, [(ps[:, 2, :], 0), (ps[:, 3, :], P)])
        pe.wait_ge(s["in"], 16 * 12)
        for i in range(2):
            nc.tensor.transpose(ps[:, 7, 16 * i:16 * i + 16], LROW[:, i, :], ident[0:16, 0:16])
        mm(ps[:, 7, 32:48], half[:], ls2[:]).then_inc(s["par_t"], 1)
        un(2, [(ps[:, 4, :], 0), (ps[:, 5, :], P)])
        un(3, [(ps[:, 6, :], 0)], w=P)
        pe.wait_ge(s["u_ev"], 4)
        un(4, [(ps[:, 0, :], 0), (ps[:, 1, :], P)])
        un(5, [(ps[:, 2, :], 0)], w=P)
        pe.wait_ge(s["sq_ev"], 10)
        pe.wait_ge(s["par_t"], 2)
        for c, tiles in enumerate(((0, 1, 2), (3, 4))):
            for j in range(TT):
                for q in tiles:
                    last = mm(ps[:, 7, 64 + 4 * c + j:65 + 4 * c + j], SQC[:, q, j * P:(j + 1) * P], ones[:, 0:1],
                              q == tiles[0], q == tiles[-1])
        last.then_inc(s["stats"], 1)
        pe.wait_ge(s["k_ev"], 1)
        mm(ps[r, 2, :], perm[r, r], KRS[r, :]).then_inc(s["rot"], 1)
        for c in range(2):
            pe.wait_ge(s["dg"], c + 1)
            mm(ps[:, 3 + c, :], ones[:], DGC[:, c, :]).then_inc(s["bc"], 1)
        for g in range(2):
            n = nu + 6 + g
            if g == 0:
                pe.wait_ge(s["rope_done"], 1)
            else:
                pe.wait_ge(s["cn"], 5)
            wk = (lambda k: pe.wait_ge(s["cl"], k + 1)) if g == 0 else None
            unit(pe, n, n % 2, [(ps[0:96, QB[4 * g + h], :], 96 * h) for h in range(4)], lambda k: CQH[:, k, :],
                 lambda k: CQL[:, k, :], range(3), 384, wait_k=wk, rows=96)
        for h in range(NH):
            pe.wait_ge(s["q_ev"], h + 1)
            mm(ps[r, QB[h], :], perm[r, r], Q[r, h, :]).then_inc(s["rot"], 1)
        n = nu + 8
        pe.wait_ge(S["split_ready"], n + 1)
        pe.wait_ge(s["cl"], 5)
        for h in range(NH):
            pe.wait_ge(s["rope_done"], h + 2)
            for k in range(2):
                ws = slice(1024 * k + P * h, 1024 * k + P * h + P)
                last = three(ps[:, QB[h], :], WH[:, n % 2, ws], WL[:, n % 2, ws], CKH[:, k, :], CKL[:, k, :], k == 0, k == 1)
            last.then_inc(s["k_mm"], 1)
        for j in range(TT):
            pe.wait_ge(s["k_ev"], j + 2)
            for k in range(2):
                wh, wl = (w[:, n % 2, 1024 * k:1024 * (k + 1)].rearrange("p (h n) -> p h n", n=P)[:, :, 64:P] for w in (WH, WL))
                o = ps[:, QB[j], :].rearrange("p (h n) -> p h n", n=64)
                ts = slice(j * P, (j + 1) * P)
                mm(o, CKH[:, k, ts], wh, k == 0, False)
                mm(o, CKL[:, k, ts], wh, False, False)
                last = mm(o, CKH[:, k, ts], wl, False, k == 1)
        last.then_inc(S["unit_done"], 1)
        pe.wait_ge(s["params"], 1)
        pe.wait_ge(s["k_ev"], 9)
        for i in range(2):
            for c in range(4):
                last = nc.tensor.transpose(ps[:, 6 + i, c * P:(c + 1) * P],
                                           BX[:, i, 4 * c:4 * c + 4, :].rearrange("p a n -> p (a n)"), ident[:])
            last.then_inc(s["bt_t"], 1)
        for i in range(2):
            for c in range(4):
                last = nc.tensor.transpose(ps[:, 3 + i, c * P:(c + 1) * P], CX[:, i, c, :], ident[:])
            last.then_inc(s["bt_t"], 1)

        def states_in(t):
            c, q = t // 4, t % 4
            rows = slice(32 * q, 32 * q + 32)
            pe.wait_ge(s["bu_taken"], t) if t else pe.wait_ge(s["bt_done"], 4)
            for i in range(2):
                mm(ps[:, 3 + i, :], BT[rows, i, c * P:(c + 1) * P], U[rows, c, :]).then_inc(s["bu"], 1)

        def states_out(t):
            c, q = t // 4, t % 4
            pe.wait_ge(s["x"], t + 1)
            if q == 0 and c:
                pe.wait_ge(s["y"], c)
            rows = slice(32 * q, 32 * q + 32)
            mm(ps[rows, 5, :], CT[:, 0, c * P + 32 * q:c * P + 32 * q + 32], VR[:], True, False)
            mm(ps[rows, 5, :], CT[:, 1, c * P + 32 * q:c * P + 32 * q + 32], VI[:], False, True).then_inc(s["yc"], 1)

        def scores(h):
            if h:
                pe.wait_ge(s["p_ready"], 4 * h)
            else:
                pe.wait_ge(s["rope_done"], 9)
                pe.wait_ge(s["k_ev"], 21)
            fl = flat(ps, 0)
            for i in order:
                o, k0, nk = CAUSAL[i]
                mm(fl[:, o:o + nk * P], Q[0:96, h, i * P:(i + 1) * P], K[0:96, h, 0:nk * P], True, False)
                last = mm(fl[:, o + i * P:o + nk * P], ident[:], cmask[:], False, True)
            last.then_inc(s["scores"], 1)

        states_in(0)
        scores(0)
        for h in range(NH):
            pe.wait_ge(s["comb"], 4 * h + 4)
            for j in range(TT):
                if j >= 2:
                    pe.wait_ge(s["pt_ready"], 4 * h + j - 1)
                elif h:
                    pe.wait_ge(s["o_hi"], 2 * h)
                    pe.wait_ge(s["pt_ready"], 4 * h)
                for i in range(j, TT):
                    o, _, _ = CAUSAL[i]
                    last = nc.tensor.transpose(ps[:, 6 + j % 2, (i - j) * P:(i - j + 1) * P],
                                               PR[:, h % 2, o + j * P:o + (j + 1) * P], ident[:])
                last.then_inc(s["tr"], 1)
            if h + 1 < NH:
                scores(h + 1)
            pe.wait_ge(s["pt_ready"], 4 * h + 4)
            rows = slice(64 * (h % 2), 64 * (h % 2) + 64)
            for j in range(TT):
                last = mm(ps[rows, 6, j * P:512], V[:, j, 64 * h:64 * h + 64], PT[:, PTO[j]:PTO[j] + (4 - j) * P], j == 0, j == 3)
            last.then_inc(s["o_ready"], 1)
            for t in (2 * h, 2 * h + 1):
                if t + 1 < 16:
                    states_in(t + 1)
                states_out(t)
        n = nu + 9
        pe.wait_ge(s["gl"], 4)
        pe.wait_ge(s["o_hi"], 16)
        unit(pe, n, n % 2, [(ps[:, c, :], c * P) for c in range(4)], lambda k: GH[:, k, :], lambda k: GL[:, k, :], range(4), 512)
        outproj_pe(pe, b, e, nu + 10, lambda k: pe.wait_ge(s["cl"], min(k, 3) + 6), XHk, XLk)

    def act(act, own, e):
        own.knows(s)
        A = nc.scalar.activation
        nu = e["nu"]
        act.wait_ge(S["x_ready"], 8 * e["x"] + 8)
        act.dma_start(PI[:], io["positions"].to_broadcast([P, T])).then_inc(s["in"], 16)
        for dst, name, rr in ((perm[:], "perm32", P), (cmask[:], "chunk", P), (half[:], "half", 2), (PAR, "par", P)):
            a, n = CONSTS[name]
            act.dma_start(dst, io["constants"][0:rr, a:a + n]).then_inc(s["in"], 16)
        a, n = CONSTS["freq"]
        act.dma_start(FREQ, io["constants"][:, a:a + n]).then_inc(s["in"], 16)
        for i, name in enumerate(("od_lam_re", "od_lam_im")):
            act.dma_start(LROW[:, i, :], io[name][0].rearrange("(t g) p -> t (g p)", g=2)).then_inc(s["in"], 16)
        for g in range(2):
            with nc.allow_non_contiguous_dma(reason="16 numbers"):
                act.dma_start(ls2[g:g + 1, :], io["od_log_step"].rearrange("a (t g) -> a g t", g=2)[:, g, :]).then_inc(s["in"], 16)
        for i, name in enumerate(("od_b_re", "od_b_im")):
            act.dma_start(BIN[:, i, :, :], io[name][0].rearrange("(t g) p h -> (g p) t h", g=2)).then_inc(s["in"], 16)
        for t in range(4):
            act.wait_ge(S["unit_done"], done_at(nu + t // 2))
            A(U[:, t, :], ps[:, t, :], ACT.Copy).then_inc(s["u_ev"], 1)
        act.wait_ge(s["par_t"], 2)
        own(A(DE, DE, ACT.Exp), "exp_in")
        act.wait_ge(s["angle_ready"], 1)
        own(A(ER, ER, ACT.Exp), "exp_in")
        act.wait_ge(s["angle_ready"], 3)
        own(A(SN, SN, ACT.Sin), "trig")
        own(A(CS, CS, ACT.Sin), "trig")
        act.wait_ge(s["angle_ready"], 4)
        own(A(SIN[:], ANG[3][:], ACT.Sin), "trig")
        act.wait_ge(s["angle_ready"], 5)
        own(A(COS[:], ANG[0][:], ACT.Sin), "trig")
        for i, name in enumerate(("od_c_re", "od_c_im")):
            act.dma_start(CIN[:, i, :, :], io[name][0].rearrange("(c g) h p -> (g h) c p", g=8)).then_inc(s["c_in"], 16)
        for q, (bank, u) in enumerate(((4, 2), (5, 2), (6, 3), (0, 4), (1, 4))):
            act.wait_ge(S["unit_done"], done_at(nu + u))
            A(RAWC[:, q, :], ps[:, bank, :], ACT.Copy).then_inc(s["sq_ev"], 1)
            A(SQC[:, q, :], ps[:, bank, :], ACT.Square).then_inc(s["sq_ev"], 1)
        act.wait_ge(S["unit_done"], done_at(nu + 5))
        A(KRS[r, :], ps[r, 2, :], ACT.Copy).then_inc(s["k_ev"], 1)
        for q in range(5):
            act.wait_ge(s["cn"], q + 1)
            dst = CQH[:, q, :] if q < 3 else CKH[:, q - 3, :]
            A(dst, CN[:, q % 2, :], ACT.Copy).then_inc(s["hi"], 1)
        for h in range(NH):
            act.wait_ge(S["unit_done"], done_at(nu + 6 + h // 4))
            A(Q[0:96, h, :], ps[0:96, QB[h], :], ACT.Copy).then_inc(s["q_ev"], 1)
        for h in range(NH):
            act.wait_ge(s["k_mm"], h + 1)
            if h == 0:
                act.wait_ge(s["cn"], 5)
            A(K[0:64, h, :], ps[0:64, QB[h], :], ACT.Copy).then_inc(s["k_ev"], 1)
        act.wait_ge(s["rope_done"], 1)
        for h in range(NH):
            A(K[r, h, :], KR[r, :], ACT.Copy).then_inc(s["k_ev"], 1)
        act.wait_ge(s["k_ev"], 17)
        act.wait_ge(S["unit_done"], done_at(nu + 8))
        for j in range(TT):
            A(V[:, j, :], ps[:, QB[j], :], ACT.Copy).then_inc(s["k_ev"], 1)

        def exps(h):
            act.wait_ge(s["max_ready"], h + 1)
            if h >= 2:
                act.wait_ge(s["tr"], 4 * (h - 1))
            for q, i in enumerate(order):
                o, _, nk = CAUSAL[i]
                z = 4 * (h % 2) + q
                A(PR[:, h % 2, o:o + nk * P], flat(ps, 0)[:, o:o + nk * P], ACT.Exp, scale=SCALE, bias=NM[:, z:z + 1],
                  accum_out=L[:, z:z + 1]).then_inc(s["p_ready"], 1)

        def gelu_tanh(c):
            act.wait_ge(s["th"], 2 * c + 1)
            own.n["th"] = 2 * c + 1
            own(A(TB[:], TB[:], ACT.Tanh, scale=0.7978845608028654), "th")

        exps(0)
        for h in range(NH):
            for j in range(TT):
                act.wait_ge(s["tr"], 4 * h + j + 1)
                A(PT[:, PTO[j]:PTO[j] + (4 - j) * P], ps[:, 6 + j % 2, 0:(4 - j) * P], ACT.Copy).then_inc(s["pt_ready"], 1)
            if h + 1 < NH:
                exps(h + 1)
            act.wait_ge(s["o_ready"], h + 1)
            rows = slice(64 * (h % 2), 64 * (h % 2) + 64)
            A(XH[rows, 4 + h // 2, :], ps[rows, 6, :], ACT.Copy).then_inc(s["o_hi"], 1)
            if h % 2:
                gelu_tanh(h // 2)
        act.wait_ge(s["gh"], 4)
        own.n["gh"] = 4
        for c in range(4):
            own(A(GH[:, c, :], U[:, c, :], ACT.Copy), "gh")
        for c in range(4):
            act.wait_ge(S["unit_done"], done_at(nu + 9))
            A((VR, VI, ZR, ZI)[c][:], ps[:, c, :], ACT.Tanh, scale=0.5, bias=BG[:, c:c + 1]).then_inc(s["p_ready"], 1)
        for c in range(4):
            act.wait_ge(s["yc"], 17 + c)
            A(XH[:, c, :], (VR, VI, ZR, ZI)[c][:], ACT.Copy, scale=0.5).then_inc(s["hi"], 1)
        b["square_act"](act, e)

    def dve(dve, own, e, residual):
        v = nc.vector
        own.knows(s)
        nu = e["nu"]
        dve.wait_ge(S["x_ready"], 8 * e["x"] + 8)
        own(v.tensor_scalar(BG, b["VEC"][:, b["vec_col"]["b_glu"]:b["vec_col"]["b_glu"] + 4], 0.5, None, ALU.mult))
        dve.wait_ge(s["par_t"], 1)
        own.n["par_t"] = 1
        for q, dst in enumerate((LR, LI, DE)):
            own(v.tensor_copy(dst, ps[:, 7, 16 * q:16 * q + 16]), "par_t" if q == 2 else None)
        dve.wait_ge(s["exp_in"], 1)
        own(v.tensor_tensor(ER, LR, DE, ALU.mult), "angle_ready")
        own(v.tensor_tensor(IM, LI, DE, ALU.mult))
        reduce_angle(nc, own, IM, XA, XK, SN, CS)
        dve.wait_ge(s["in"], 16 * 12)
        rope_angles(nc, own, PI[:], PF[:], [a[:] for a in ANG], FREQ[:, 1:2])
        dve.wait_ge(s["trig"], 2)
        dve.wait_ge(s["exp_in"], 2)
        own(v.tensor_tensor(XA, ER, CS, ALU.mult))
        own(v.tensor_scalar(XA, XA, -1.0, None, ALU.add))
        own(v.tensor_tensor(XK, ER, SN, ALU.mult))
        own(v.tensor_tensor(XB, LR, LR, ALU.mult))
        own(v.tensor_tensor(T0, LI, LI, ALU.mult))
        own(v.tensor_tensor(XB, XB, T0, ALU.add))
        own(v.reciprocal(XB, XB))
        own(v.tensor_tensor(FR, XA, LR, ALU.mult))
        own(v.tensor_tensor(T0, XK, LI, ALU.mult))
        own(v.tensor_tensor(FR, FR, T0, ALU.add))
        own(v.tensor_tensor(FR, FR, XB, ALU.mult))
        own(v.tensor_tensor(FI, XK, LR, ALU.mult))
        own(v.tensor_tensor(T0, XA, LI, ALU.mult))
        own(v.tensor_tensor(FI, FI, T0, ALU.subtract))
        own(v.tensor_tensor(FI, FI, XB, ALU.mult))
        wide = lambda a: a[:, :, None].to_broadcast([P, 16, 16])
        TMP = CN[:, 0, 0:256].rearrange("p (a n) -> p a n", n=16)
        for i, (x, y, op) in enumerate(((0, 1, ALU.subtract), (1, 0, ALU.add))):
            own(v.tensor_tensor(BB[:, i], BIN[:, x], wide(FR), ALU.mult))
            own(v.tensor_tensor(TMP, BIN[:, y], wide(FI), ALU.mult))
            own(v.tensor_tensor(BB[:, i], BB[:, i], TMP, op))
        dve.wait_ge(s["trig"], 4)
        for i in range(2):
            for g in range(2):
                own(v.tensor_scalar(BX[:, i, :, 16 * g:16 * g + 16], BB[:, i], PAR[:, g:g + 1], None, ALU.mult))
        dve.wait_ge(s["c_in"], 32)
        for i in range(2):
            for g in range(2):
                m = PAR[:, 2 + g:3 + g]
                own(v.tensor_scalar(CX[:, i, :, 64 * g:64 * g + 64], CIN[:, i], m, -1.0 if i else 1.0, ALU.mult, ALU.mult),
                    "params" if i and g else None)
        dve.wait_ge(s["stats"], 1)
        own(v.tensor_scalar(SS[:, 0:4], ps[:, 7, 64:68], 1.0 / 384, RMS_EPS, ALU.mult, ALU.add))
        own(v.tensor_scalar(SS[:, 4:8], ps[:, 7, 68:72], 1.0 / 256, RMS_EPS, ALU.mult, ALU.add))
        rsqrt(own, SS, RS, TMPA)
        for c in range(2):
            own(v.tensor_tensor(DGC[:, c, :].rearrange("p (j n) -> p j n", n=P), ident[:, None, :].to_broadcast([P, TT, P]),
                                RS[:, 4 * c:4 * c + 4][:, :, None].to_broadcast([P, TT, P]), ALU.mult), "dg")
        dve.wait_ge(s["rot"], 1)
        own(v.tensor_tensor(AB[r, 0, :], KRS[r, :], COS[r, :], ALU.mult))
        own(v.tensor_tensor(AB[r, 1, :], ps[r, 2, :], SIN[r, :], ALU.mult))
        own(v.tensor_tensor(KR[r, :], AB[r, 0, :], AB[r, 1, :], ALU.add), "rope_done")
        dve.wait_ge(s["bc"], 2)

        def cn(q):
            g = vcol("q_norm", q) if q < 3 else vcol("kv_norm", q - 3)
            own(v.scalar_tensor_tensor(CN[:, q % 2, :], RAWC[:, q, :], g, ps[:, 3 if q < 3 else 4, :], ALU.mult, ALU.mult), "cn")

        cn(0)
        for q in range(5):
            if q < 4:
                cn(q + 1)
            dve.wait_ge(s["hi"], q + 1)
            h, l = (CQH[:, q, :], CQL[:, q, :]) if q < 3 else (CKH[:, q - 3, :], CKL[:, q - 3, :])
            own(v.tensor_tensor(l, CN[:, q % 2, :], h.bitcast(F32), ALU.subtract), "cl")
        for h in range(NH):
            dve.wait_ge(s["rot"], h + 2)
            own(v.tensor_tensor(AB[r, 0, :], Q[r, h, :], COS[r, :], ALU.mult), wait=False)
            own(v.tensor_tensor(AB[r, 1, :], ps[r, QB[h], :], SIN[r, :], ALU.mult))
            own(v.tensor_tensor(Q[r, h, :], AB[r, 0, :], AB[r, 1, :], ALU.add), "rope_done")
        dve.wait_ge(s["bc"], 2)
        for q in range(4):
            dve.wait_ge(s["bt_t"], q + 1)
            own(v.tensor_copy((BT if q < 2 else CT)[:, q % 2, :], ps[:, (6, 7, 3, 4)[q], :]), "bt_done")

        def tile(t):
            c, q = t // 4, t % 4
            co, si = (TC, TS) if c % 2 else (TC1, TS1)
            co, si = co[:, q, :], si[:, q, :]
            ra = ER[:, t:t + 1].to_broadcast([P, T])
            br, bi = ps[:, 3, :], ps[:, 4, :]
            if q == 0:
                dve.wait_ge(s["table"], c + 1)
            dve.wait_ge(s["bu"], 2 * t + 2)
            own(v.tensor_tensor(TA[:], si, bi, ALU.mult), wait=False)
            own(v.tensor_tensor(TB[:], si, br, ALU.mult), wait=False)
            if t:
                dve.wait_ge(s["yc"], t)
            own(v.tensor_tensor(VR[:], co, br, ALU.mult), wait=False)
            own(v.tensor_tensor(VI[:], co, bi, ALU.mult))
            dve.sem_inc(s["bu_taken"], 1)
            own(v.tensor_tensor(VR[:], VR[:], TA[:], ALU.add), wait=False)
            own(v.tensor_tensor(VI[:], VI[:], TB[:], ALU.subtract))
            own(v.tensor_tensor_scan(TA[:], ra, VR[:], 0.0, ALU.mult, ALU.add), wait=False)
            own(v.tensor_tensor_scan(TB[:], ra, VI[:], 0.0, ALU.mult, ALU.add))
            own(v.tensor_tensor(VR[:], co, TA[:], ALU.mult), wait=False)
            own(v.tensor_tensor(VI[:], co, TB[:], ALU.mult))
            own(v.tensor_tensor(TA[:], si, TA[:], ALU.mult), wait=False)
            own(v.tensor_tensor(TB[:], si, TB[:], ALU.mult))
            own(v.tensor_tensor(VR[:], VR[:], TB[:], ALU.subtract))
            own(v.tensor_tensor(VI[:], VI[:], TA[:], ALU.add), "x")

        def gelu(c):
            dve.wait_ge(s["yc"], 4 * c + 4)
            own(v.scalar_tensor_tensor(YS[:], U[:, c, :], vcol("s5_skip", c), ps[:, 5, :], ALU.mult, ALU.add), "y")
            own(v.tensor_tensor(TB[:], YS[:], YS[:], ALU.mult))
            own(v.tensor_scalar(TB[:], TB[:], 0.044715, 1.0, ALU.mult, ALU.add))
            own.n["th"] = 2 * c
            own(v.tensor_tensor(TB[:], TB[:], YS[:], ALU.mult), "th")
            dve.wait_ge(s["th"], 2 * c + 2)
            own(v.scalar_tensor_tensor(TB[:], TB[:], 1.0, YS[:], ALU.add, ALU.mult))
            own(v.tensor_scalar(U[:, c, :], TB[:], 0.5, None, ALU.mult), "gh")

        def maxes(h):
            dve.wait_ge(s["scores"], h + 1)
            for q, i in enumerate(order):
                o, _, nk = CAUSAL[i]
                own(v.tensor_reduce(MX[:, q:q + 1], flat(ps, 0)[:, o:o + nk * P], AX.X, ALU.max), wait=q == 3)
            z = 4 * (h % 2)
            own(v.tensor_scalar(NM[:, z:z + 4], MX, -SCALE, None, ALU.mult), "max_ready")

        maxes(0)
        for h in range(NH):
            dve.wait_ge(s["p_ready"], 4 * h + 4)
            z = 4 * (h % 2)
            own(v.reciprocal(RC, L[:, z:z + 4]))
            for q, i in enumerate(order):
                o, _, nk = CAUSAL[i]
                p1 = PR[:, h % 2, o:o + nk * P]
                own(v.tensor_scalar(p1, p1, RC[:, q:q + 1], None, ALU.mult), "comb", wait=q == 3)
            tile(2 * h)
            if h + 1 < NH:
                maxes(h + 1)
            dve.wait_ge(s["o_hi"], 2 * h + 1)
            rows = slice(64 * (h % 2), 64 * (h % 2) + 64)
            own(v.tensor_tensor(XL[rows, 4 + h // 2, :], ps[rows, 6, :], XH[rows, 4 + h // 2, :].bitcast(F32), ALU.subtract))
            dve.sem_inc(s["o_hi"], 1)
            tile(2 * h + 1)
            if h % 2:
                gelu(h // 2)
        for c in range(4):
            dve.wait_ge(s["gh"], 5 + c)
            own(v.tensor_tensor(GL[:, c, :], U[:, c, :], GH[:, c, :].bitcast(F32), ALU.subtract), "gl")
        yb = (VR, VI, ZR, ZI)
        own.n["yc"] = 16
        for c in range(4):
            dve.wait_ge(s["p_ready"], 33 + c)
            own(v.scalar_tensor_tensor(yb[c][:], yb[c][:], 1.0, U[:, c, :], ALU.add, ALU.mult), "yc")
        for c in range(4):
            dve.wait_ge(s["hi"], 6 + c)
            own(v.scalar_tensor_tensor(XL[:, c, :], yb[c][:], 0.5, XH[:, c, :].bitcast(F32), ALU.mult, ALU.subtract), "cl")
        outproj_dve(b, e, nu + 10, residual)

    def pool(pool, own, e, split_units, done):
        g = nc.gpsimd
        own.knows(dict(table=s["table"]))

        def table(c, begin, end):
            tc, ts = (TC, TS) if c % 2 else (TC1, TS1)
            if begin == 1:
                if c == 0:
                    pool.wait_ge(S["unit_done"], done_at(e["nu"] + 5))
                    pool.wait_ge(s["trig"], 2)
                elif c == 1:
                    pool.wait_ge(s["bt_t"], 4)
                else:
                    pool.wait_ge(s["x"], 4 * (c - 1))
                own(g.memset(tc[:, :, 0:1], 1.0), wait=False)
                own(g.memset(ts[:, :, 0:1], 0.0), wait=False)
                own(g.tensor_copy(W2[:, 0, 0:4], CS[:, 4 * c:4 * c + 4]), wait=False)
                own(g.tensor_copy(W2[:, 1, 0:4], SN[:, 4 * c:4 * c + 4]))
            m = begin
            while m < end:
                wr, wi = (W2[:, i, 0:4][:, :, None].to_broadcast([P, 4, m]) for i in range(2))
                t = SCR[c >= 2, m][:]
                lo, hi = slice(0, m), slice(m, 2 * m)
                own(g.tensor_tensor(tc[:, :, hi], tc[:, :, lo], wr, ALU.mult), wait=False)
                own(g.tensor_tensor(t, ts[:, :, lo], wi, ALU.mult))
                own(g.tensor_tensor(tc[:, :, hi], tc[:, :, hi], t, ALU.subtract), wait=False)
                own(g.tensor_tensor(ts[:, :, hi], ts[:, :, lo], wr, ALU.mult))
                own(g.tensor_tensor(t, tc[:, :, lo], wi, ALU.mult))
                own(g.tensor_tensor(ts[:, :, hi], ts[:, :, hi], t, ALU.add), "table" if 2 * m == T else None)
                m *= 2
                if m < T:
                    own(g.tensor_tensor(W2[:, 0, 4:8], W2[:, 0, 0:4], W2[:, 1, 0:4], ALU.mult), wait=False)
                    own(g.tensor_tensor(W2[:, 1, 4:8], W2[:, 1, 0:4], W2[:, 1, 0:4], ALU.mult))
                    own(g.tensor_tensor(W2[:, 0, 0:4], W2[:, 0, 0:4], W2[:, 0, 0:4], ALU.mult))
                    own(g.tensor_tensor(W2[:, 0, 0:4], W2[:, 0, 0:4], W2[:, 1, 4:8], ALU.subtract), wait=False)
                    own(g.tensor_scalar(W2[:, 1, 0:4], W2[:, 0, 4:8], 2.0, 0.0, ALU.mult, ALU.add))

        split_units(done, e["table_at"])
        table(0, 1, T // 2)
        split_units(e["table_at"], e["table_at"] + 2)
        table(0, T // 2, T)
        split_units(e["table_at"] + 2, e["pool_at"])
        for c in range(1, 4):
            table(c, 1, T)

    return dict(pe=pe, act=act, dve=dve, pool=pool)





def window_mixer(nc, b):
    S, ps, sb, sem, WORK, WORK2 = (b[k] for k in ("S", "ps", "sb", "sem", "WORK", "WORK2"))
    ident, ones, io, done_at, XHk, XLk = (b[k] for k in ("ident", "ones", "io", "unit_done_at", "XHk", "XLk"))
    XH, XL, WH, WL = (b[k] for k in ("XH", "XL", "WH", "WL"))
    KB = 1024
    NH, HD = 16, 64
    SCALE = HD ** -0.5
    Q = sb("wa_q", [P, 8, T], at=WORK)
    K = sb("wa_k", [P, 4, T], at=WORK + 16 * KB)
    V = sb("wa_v", [P, TT, 256], at=WORK + 24 * KB)
    SLOPES = sb("wa_slopes", [P, NH, P], at=WORK + 28 * KB)
    PR = sb("wa_p", [P, 2, 3 * T], at=WORK + 36 * KB)
    PT = sb("wa_pt", [P, 3 * T], at=WORK + 48 * KB)
    dist = sb("wa_dist", [P, 3 * P], at=WORK + 54 * KB)
    cst = sb("wa_cst", [P, 32], at=WORK + 56 * KB)
    sm = sb("wa_small", [P, 64], at=WORK + 57 * KB)
    SLOPE, SINK = cst[:, 0:16], cst[:, 16:32]
    MX, NM, L, ES, RC = sm[:, 0:4], sm[:, 4:12], sm[:, 12:20], sm[:, 20:28], sm[:, 28:32]
    s = {n: sem("wa_" + n) for n in "in slopes ev scores max_ready p_ready comb tr pt_ready o_ready o_hi".split()}
    order = [1, 2, 0, 3]

    def pe(pe, e):
        mm = b["mm"]
        n = e["nv"]
        pe.wait_ge(S["split_ready"], n + 1)
        for k in range(KD):
            pe.wait_ge(S["x_ready"], 8 * e["x"] + k + 1)
            for j in range(TT):
                ws, ts = slice(256 * k, 256 * k + 256), slice(P * j, P * j + P)
                mm(ps[:, j, 0:256], XH[:, k, ts], WH[:, n % 2, ws], k == 0, False)
                mm(ps[:, j, 0:256], XL[:, k, ts], WH[:, n % 2, ws], False, False)
                last = mm(ps[:, j, 0:256], XH[:, k, ts], WL[:, n % 2, ws], False, k == KD - 1)
        last.then_inc(S["unit_done"], 1)
        for u in range(5):
            bank = (4, 6, 0, 2, 4)[u]
            if u >= 2:
                pe.wait_ge(s["ev"], (4, 4, 12)[u - 2])
            b["fm_unit"](pe, n + 1 + u, (n + 1 + u) % 2, [(ps[:, bank, :], 0), (ps[:, bank + 1, :], P)], XHk, XLk, range(8), 256)

        def scores(h):
            c = h % 2
            if h >= 2:
                pe.wait_ge(s["p_ready"], 5 * (h - 1))
            elif h == 0:
                pe.wait_ge(s["slopes"], 1)
                pe.wait_ge(s["ev"], 20)
            fl, rows = flat(ps, 3 * c), slice(64 * (h % 2), 64 * (h % 2) + 64)
            for i in order:
                o, k0, nk = BANDED[i]
                d0 = (k0 - i + 1) * P
                mm(fl[:, o:o + nk * P], Q[rows, h // 2, i * P:(i + 1) * P], K[rows, h // 4, k0 * P:(k0 + nk) * P], True, False)
                last = mm(fl[:, o:o + nk * P], SLOPES[:, h, :], dist[:, d0:d0 + nk * P], False, True)
            last.then_inc(s["scores"], 1)

        scores(0)
        for h in range(NH):
            if h + 1 < NH:
                scores(h + 1)
            pe.wait_ge(s["comb"], 4 * h + 4)
            for q, i in enumerate(order):
                if q >= 2:
                    pe.wait_ge(s["pt_ready"], 4 * h + q - 1)
                elif h:
                    pe.wait_ge(s["o_hi"], 2 * h)
                    pe.wait_ge(s["pt_ready"], 4 * h)
                o, k0, nk = BANDED[i]
                for m in range(nk):
                    last = nc.tensor.transpose(ps[:, 6 + q % 2, m * P:(m + 1) * P], PR[:, h % 2, o + m * P:o + (m + 1) * P], ident[:])
                last.then_inc(s["tr"], 1)
            pe.wait_ge(s["pt_ready"], 4 * h + 4)
            rows, kv = slice(64 * (h % 2), 64 * (h % 2) + 64), h // 4
            for i in range(TT):
                o, k0, nk = BANDED[i]
                for m in range(nk):
                    last = mm(ps[rows, 6, i * P:(i + 1) * P], V[:, k0 + m, HD * kv:HD * kv + HD], PT[:, o + m * P:o + (m + 1) * P],
                              m == 0, m == nk - 1)
            last.then_inc(s["o_ready"], 1)
        outproj_pe(pe, b, e, e["no"], lambda k: pe.wait_ge(s["o_hi"], 2 * NH), XHk, XLk)

    def act(act, own, e):
        own.knows(s)
        A = nc.scalar.activation
        act.wait_ge(S["x_ready"], 8 * e["x"] + 8)
        for dst, name in ((dist[:], "window"), (SLOPE, "slope")):
            a, n = CONSTS[name]
            act.dma_start(dst, io["constants"][:, a:a + n]).then_inc(s["in"], 16)
        act.dma_start(SINK, io["at_sink_2"].to_broadcast([P, NH])).then_inc(s["in"], 16)
        act.wait_ge(S["unit_done"], done_at(e["nv"]))
        for j in range(TT):
            A(V[:, j, :], ps[:, j, 0:256], ACT.Copy).then_inc(s["ev"], 1)
        act.wait_ge(S["unit_done"], done_at(e["nv"] + 1))
        for kv in range(4):
            for half in range(2):
                A(K[64 * half:64 * half + 64, kv, :], ps[64 * (kv % 2):64 * (kv % 2) + 64, 4 + kv // 2, :], ACT.Copy)\
                    .then_inc(s["ev"], 1)
        for t in range(8):
            act.wait_ge(S["unit_done"], done_at(e["nv"] + 2 + t // 2))
            A(Q[:, t, :], ps[:, (6, 7, 0, 1, 2, 3, 4, 5)[t], :], ACT.Copy).then_inc(s["ev"], 1)

        def exps(h):
            act.wait_ge(s["max_ready"], h + 1)
            if h >= 2:
                act.wait_ge(s["tr"], 4 * (h - 1))
            for q, i in enumerate(order):
                o, _, nk = BANDED[i]
                z = 4 * (h % 2) + q
                A(PR[:, h % 2, o:o + nk * P], flat(ps, 3 * (h % 2))[:, o:o + nk * P], ACT.Exp, scale=SCALE, bias=NM[:, z:z + 1],
                  accum_out=L[:, z:z + 1]).then_inc(s["p_ready"], 1)
            z = 4 * (h % 2)
            A(ES[:, z:z + 4], NM[:, z:z + 4], ACT.Exp, bias=SINK[:, h:h + 1]).then_inc(s["p_ready"], 1)

        exps(0)
        for h in range(NH):
            for q, i in enumerate(order):
                o, _, nk = BANDED[i]
                act.wait_ge(s["tr"], 4 * h + q + 1)
                A(PT[:, o:o + nk * P], ps[:, 6 + q % 2, 0:nk * P], ACT.Copy).then_inc(s["pt_ready"], 1)
            if h + 1 < NH:
                exps(h + 1)
            act.wait_ge(s["o_ready"], h + 1)
            rows = slice(64 * (h % 2), 64 * (h % 2) + 64)
            A(XH[rows, h // 2, :], ps[rows, 6, :], ACT.Copy).then_inc(s["o_hi"], 1)
        b["square_act"](act, e)

    def dve(dve, own, e, residual):
        v = nc.vector
        own.knows(s)
        dve.wait_ge(s["in"], 48)
        own(v.tensor_tensor(SLOPES[:], ident[:, None, :].to_broadcast([P, NH, P]), SLOPE[:, :, None].to_broadcast([P, NH, P]),
                            ALU.mult), "slopes")

        def maxes(h):
            dve.wait_ge(s["scores"], h + 1)
            fl = flat(ps, 3 * (h % 2))
            own(v.tensor_reduce(MX[:, 0:2], fl[:, 0:1024].rearrange("p (a n) -> p a n", n=512)[:, :, 0:384], AX.X, ALU.max),
                wait=False)
            own(v.tensor_reduce(MX[:, 2:4], fl[:, 1024:1536].rearrange("p (a n) -> p a n", n=256), AX.X, ALU.max))
            z = 4 * (h % 2)
            own(v.tensor_scalar(MX, MX, SCALE, SINK[:, h:h + 1], ALU.mult, ALU.max))
            own(v.tensor_scalar(NM[:, z:z + 4], MX, -1.0, None, ALU.mult), "max_ready")

        maxes(0)
        for h in range(NH):
            dve.wait_ge(s["p_ready"], 5 * h + 5)
            z = 4 * (h % 2)
            own(v.tensor_tensor(RC, L[:, z:z + 4], ES[:, z:z + 4], ALU.add))
            own(v.reciprocal(RC, RC))
            for q, i in enumerate(order):
                o, _, nk = BANDED[i]
                p1 = PR[:, h % 2, o:o + nk * P]
                own(v.tensor_scalar(p1, p1, RC[:, q:q + 1], None, ALU.mult), "comb", wait=q == 3)
            if h + 1 < NH:
                maxes(h + 1)
            dve.wait_ge(s["o_hi"], 2 * h + 1)
            rows = slice(64 * (h % 2), 64 * (h % 2) + 64)
            own(v.tensor_tensor(XL[rows, h // 2, :], ps[rows, 6, :], XH[rows, h // 2, :].bitcast(F32), ALU.subtract))
            dve.sem_inc(s["o_hi"], 1)
        outproj_dve(b, e, e["no"], residual)

    return dict(pe=pe, act=act, dve=dve)


def mlstm_mixer(nc, b):
    S, ps, sb, sem, WORK, WORK2 = (b[k] for k in ("S", "ps", "sb", "sem", "WORK", "WORK2"))
    ident, ones, io, vcol, done_at, XHk, XLk = (b[k] for k in ("ident", "ones", "io", "vcol", "unit_done_at", "XHk", "XLk"))
    XH, XL, WH, WL = (b[k] for k in ("XH", "XL", "WH", "WL"))
    KB = 1024
    NH, DV = 4, 256
    KSCALE = 128 ** -0.5
    Q = sb("ml_q", [P, NH, T], at=WORK)
    K = sb("ml_k", [P, NH, T], at=WORK + 8 * KB)
    V = sb("ml_v", [P, TT, D], at=WORK + 16 * KB)
    SIG = sb("ml_sig", [P, 8, T], at=WORK + 32 * KB)
    H = sb("ml_h", [P, 8, T], at=WORK + 48 * KB)
    HSQ = sb("ml_hsq", [P, 8, T], at=b["XH_AT"] + 16 * KB)
    E = sb("ml_e", [P, 2, 2, 1280], at=WORK + 64 * KB)
    NM = sb("ml_nm", [64, T], at=WORK + 84 * KB)
    EM = sb("ml_em", [64, T], at=WORK + 86 * KB)
    GT, F, I, G, U1, U2, U3, EE, M, C = (sb(f"ml_row{i}", [64, T], at=WORK + (64 + 2 * i) * KB) for i in range(10))
    DG = sb("ml_dg", [P, 2, 2, T], at=WORK + 64 * KB)
    tri = sb("ml_tri", [P, P], at=WORK2 + 4 * KB)
    trir = sb("ml_trir", [P, P], at=WORK2 + 4 * KB + 512)
    CC = sb("ml_cc", [P, 256], at=WORK2 + 5 * KB)
    gb = sb("ml_gb", [16, 1], at=WORK2 + 6 * KB)
    gain = sb("ml_gain", [P, 8], at=WORK2 + 6 * KB + 32)
    tm = sb("ml_tm", [P, 6, 16], at=WORK2 + 6 * KB + 64)
    MU, VAR, RS, TMPA, NB, _ = (tm[:, i, :] for i in range(6))
    QK = sb("ml_qk", [P, TT, T], at=WORK2 + 8 * KB)
    RC = sb("ml_rc", [P, T], at=WORK2 + 16 * KB)
    YT = sb("ml_yt", [P, 2, T], at=WORK2 + 8 * KB)
    s = {n: sem("ml_" + n) for n in "in ev gt sel x e rows bcast exp st m den sc hv hev dg bc y".split()}
    FCOL = {0: 0, 1: 512, 3: 896, 2: 1024}
    BCOL = {3: 0, 2: 512, 0: 896, 1: 1024}

    def span(d, i):
        return (FCOL[i], FCOL[i] + (4 - i) * P, i * P, T) if d == 0 else (BCOL[i], BCOL[i] + (i + 1) * P, 0, (i + 1) * P)

    def pe(pe, e):
        mm = b["mm"]
        n0 = e["n0"]
        for h in range(2):
            if h:
                b["fm_unit"](pe, n0 + 2, n0 % 2, [(ps[:, 7, :], 0)], XHk, XLk, range(8), P)
                pe.wait_ge(s["ev"], 4)
            for g in range(2):
                n = n0 + 3 * h + g
                pe.wait_ge(S["split_ready"], n + 1)
                for q in range(4):
                    k = 4 * g + q
                    if h == 0:
                        pe.wait_ge(S["x_ready"], 8 * e["x"] + k + 1)
                    for j in range(TT):
                        ws, ts = slice(512 * q, 512 * q + 512), slice(P * j, P * j + P)
                        mm(ps[:, j, :], XH[:, k, ts], WH[:, n % 2, ws], k == 0, False)
                        mm(ps[:, j, :], XL[:, k, ts], WH[:, n % 2, ws], False, False)
                        last = mm(ps[:, j, :], XH[:, k, ts], WL[:, n % 2, ws], False, k == 7)
                last.then_inc(S["unit_done"], 1)
                if h == 1 and g == 0:
                    pe.wait_ge(s["gt"], 1)
                    for kind in range(2):
                        mm(ps[0:32, 4 + kind, :], ident[0:16, 4 * kind:4 * kind + 32], GT[0:16, :])
                        last = mm(ps[32:64, 4 + kind, :], ident[0:16, 8 + 4 * kind:40 + 4 * kind], GT[0:16, ::-1])
                    last.then_inc(s["sel"], 1)
        for u in range(8):
            bank = (0, 2, 6, 4)[u % 4]
            if u == 3:
                pe.wait_ge(s["x"], 1)
            elif u != 2:
                pe.wait_ge(s["ev"], (6, 8, 0, 0, 10, 12, 14, 16)[u])
            n = n0 + 5 + u
            b["fm_unit"](pe, n, n % 2, [(ps[:, bank, :], 0), (ps[:, bank + 1, :], P)], XHk, XLk, range(8), 256)
        pe.wait_ge(s["rows"], 1)
        pe.wait_ge(s["ev"], 24)
        for i in range(TT):
            last = nc.tensor.transpose(ps[:, 4, 64 * i:64 * i + 64], C[:, i * P:(i + 1) * P], ident[0:64, 0:64])
        last.then_inc(s["sel"], 1)

        def qk(h):
            for i in range(TT):
                last = mm(ps[:, i, :], K[:, h, i * P:(i + 1) * P], Q[:, h, :])
            last.then_inc(s["st"], 1)

        def spread(h, d):
            if h == 0 and d == 0:
                pe.wait_ge(s["x"], 3)
            else:
                pe.wait_ge(s["exp"], 7 * (2 * h + d))
            row = 32 * d + h
            one = ident[0:64, row:row + 1].to_broadcast([64, P])
            mm(ps[:, 4, :], one, NM[:])
            mm(ps[:, 5, :], one, NM[:], True, False)
            mask = (tri, trir)[d]
            for i in range(TT):
                last = mm(ps[:, 5, i * P:(i + 1) * P], ident[:], mask[:], False, i == 3)
            last.then_inc(s["bcast"], 1)

        def den(h, d):
            pe.wait_ge(s["m"], 8 * h + 4 * d + 4)
            if h or d:
                pe.wait_ge(s["sc"], 2 * h + d)
            row = 32 * d + h
            mm(ps[:, 7, :], ident[0:64, row:row + 1].to_broadcast([64, P]), EM[:])
            tiles = (range(4), range(3, -1, -1))[d]
            for i in tiles:
                a, z, t0, t1 = span(d, i)
                last = mm(ps[:, 6, t0:t1], ones[:], E[:, h % 2, d, a:z], i == tiles[0], i == tiles[-1])
            last.then_inc(s["den"], 1)

        def values(h):
            pe.wait_ge(s["sc"], 2 * h + 2)
            if h + 1 < NH:
                pe.wait_ge(s["ev"], 28 + 4 * (h + 1))
            else:
                pe.wait_ge(s["hev"], 4 * h)
            for c in range(2):
                pairs = [(0, i) for i in range(4)] + [(1, i) for i in range(3, 0, -1)]
                for q, (d, i) in enumerate(pairs):
                    a, z, t0, t1 = span(d, i)
                    if d:
                        z, t1 = z - P, t1 - P
                    last = mm(ps[:, c, t0:t1], V[:, i, DV * h + P * c:DV * h + P * (c + 1)], E[:, h % 2, d, a:z], q == 0, q == 6)
            last.then_inc(s["hv"], 1)

        qk(0)
        spread(0, 0)
        spread(0, 1)
        den(0, 0)
        den(0, 1)
        for h in range(NH):
            if h + 1 < NH:
                if h:
                    pe.wait_ge(s["hev"], 4 * h)
                qk(h + 1)
                spread(h + 1, 0)
                spread(h + 1, 1)
            values(h)
            if h + 1 < NH:
                den(h + 1, 0)
                den(h + 1, 1)
        pe.wait_ge(s["hev"], 16)
        pe.wait_ge(s["sc"], 8)
        for q, src in enumerate((H, HSQ)):
            for h in range(NH):
                for j in range(TT):
                    for c in range(2):
                        z = 16 * q + 4 * h + j
                        last = mm(ps[:, 6, z:z + 1], src[:, 2 * h + c, j * P:(j + 1) * P], ones[:, 0:1], c == 0, c == 1)
        last.then_inc(s["sel"], 1)
        for h in range(NH):
            pe.wait_ge(s["dg"], 2 * h + 2)
            if h >= 2:
                pe.wait_ge(s["y"], 2 * (h - 1))
            for q in range(2):
                last = mm(ps[:, 2 * (h % 2) + q, :], ones[:], DG[:, h % 2, q, :])
            last.then_inc(s["bc"], 1)
        outproj_pe(pe, b, e, n0 + 13, lambda k: pe.wait_ge(S["x_ready"], 8 * (e["x"] + 1) + k + 1), XHk, XLk)

    def act(act, own, e):
        own.knows(s)
        A = nc.scalar.activation
        n0 = e["n0"]
        act.wait_ge(S["x_ready"], 8 * e["x"] + 8)
        for dst, name in ((tri, "tri"), (trir, "tri_rev")):
            a, n = CONSTS[name]
            act.dma_start(dst[:], io["constants"][:, a:a + n]).then_inc(s["in"], 16)
        with nc.allow_non_contiguous_dma(reason="16 numbers"):
            act.dma_start(gb[:], io["ml_gate_b_2"].rearrange("a n -> n a")).then_inc(s["in"], 16)
        for h in range(2):
            if h:
                act.wait_ge(S["unit_done"], done_at(n0 + 2))
                act.wait_ge(s["in"], 48)
                A(GT[0:16, :], ps[0:16, 7, :], ACT.Identity, bias=gb[:]).then_inc(s["gt"], 1)
                act.wait_ge(s["x"], 1)
                own(A(EE[:], EE[:], ACT.Exp, scale=-1.0), "e")
            act.wait_ge(S["unit_done"], done_at(n0 + 1 + 3 * h))
            for j in range(TT):
                A(V[:, j, 512 * h:512 * h + 512], ps[:, j, :], ACT.Copy).then_inc(s["ev"], 1)
        act.wait_ge(s["x"], 2)
        own(A(EM[:], EM[:], ACT.Exp), "e")
        for t in range(16):
            u = t // 2
            act.wait_ge(S["unit_done"], done_at(n0 + 5 + u))
            src = ps[:, (0, 2, 6, 4)[u % 4] + t % 2, :]
            if t < 8:
                A((Q if t < 4 else K)[:, t % 4, :], src, ACT.Copy).then_inc(s["ev"], 1)
            else:
                A(SIG[:, t - 8, :], src, ACT.Tanh, scale=0.5).then_inc(s["ev"], 1)

        def heads_in(h):
            act.wait_ge(s["st"], h + 1)
            if h:
                act.wait_ge(s["m"], 8 * h)
            for i in range(TT):
                A(QK[:, i, :], ps[:, i, :], ACT.Copy, scale=KSCALE).then_inc(s["ev"], 1)
            for d in range(2):
                act.wait_ge(s["bcast"], 2 * h + d + 1)
                if h >= 2:
                    act.wait_ge(s["hv"], h - 1)
                for i in range(TT):
                    a, z, t0, t1 = span(d, i)
                    at = a + i * P - t0
                    bias = CC[:, 64 * i + 32 * d + h:64 * i + 32 * d + h + 1]
                    A(E[:, h % 2, d, at:at + P], ps[:, 5, i * P:(i + 1) * P], ACT.Exp, bias=bias).then_inc(s["exp"], 1)
                    if t1 - t0 > P:
                        rest = (a + P, z, t0 + P, t1) if d == 0 else (a, z - P, t0, t1 - P)
                        A(E[:, h % 2, d, rest[0]:rest[1]], ps[:, 4, rest[2]:rest[3]], ACT.Exp, bias=bias).then_inc(s["exp"], 1)

        heads_in(0)
        for h in range(NH):
            if h + 1 < NH:
                heads_in(h + 1)
            act.wait_ge(s["hv"], h + 1)
            for c in range(2):
                A(H[:, 2 * h + c, :], ps[:, c, :], ACT.Copy).then_inc(s["hev"], 1)
                A(HSQ[:, 2 * h + c, :], ps[:, c, :], ACT.Square).then_inc(s["hev"], 1)
        for k in range(8):
            act.wait_ge(s["y"], k + 1)
            A(XH[:, k, :], YT[:, k % 2, :], ACT.Copy, scale=gain[:, k:k + 1]).then_inc(s["e"], 1)
        b["square_act"](act, e)

    def dve(dve, own, e, residual):
        v = nc.vector
        own.knows(s)
        dve.wait_ge(S["x_ready"], 8 * e["x"] + 8)
        own(v.tensor_scalar(gain[:], b["VEC"][:, b["vec_col"]["ml_norm"]:b["vec_col"]["ml_norm"] + 8], 0.5, None, ALU.mult))
        dve.wait_ge(s["sel"], 1)
        own(v.tensor_copy(I[:], ps[0:64, 4, :]))
        own(v.tensor_copy(F[:], ps[0:64, 5, :]))
        own(v.scalar_tensor_tensor(EE[:], F[:], -1.0, F[:], ALU.mult, ALU.max), "x")
        dve.wait_ge(s["e"], 1)
        own(v.tensor_scalar(U1[:], EE[:], 2.0, None, ALU.add))
        own(v.reciprocal(U1[:], U1[:]))
        own(v.tensor_tensor(U1[:], U1[:], EE[:], ALU.mult))
        own(v.tensor_tensor(U2[:], U1[:], U1[:], ALU.mult))
        own(v.memset(U3[:], 1.0 / 19))
        for d in (17, 15, 13, 11, 9, 7, 5, 3, 1):
            own(v.tensor_tensor(U3[:], U3[:], U2[:], ALU.mult))
            own(v.tensor_scalar(U3[:], U3[:], 1.0 / d, None, ALU.add))
        own(v.scalar_tensor_tensor(U3[:], U3[:], 2.0, U1[:], ALU.mult, ALU.mult))
        own(v.scalar_tensor_tensor(F[:], F[:], 0.0, U3[:], ALU.min, ALU.subtract))
        one = ones[0:64, 0:1].to_broadcast([64, T])
        own(v.tensor_tensor_scan(G[:], one, F[:], 0.0, ALU.mult, ALU.add))
        own(v.tensor_tensor(I[:], I[:], G[:], ALU.subtract))
        own(v.tensor_tensor_scan(M[:], one, I[:], 0.0, ALU.mult, ALU.max))
        own(v.tensor_tensor(G[:], G[:], M[:], ALU.add))
        for rows, st in ((slice(0, 32), 1), (slice(32, 64), -1)):
            own(v.tensor_scalar(EM[rows, :], G[rows, ::st], -1.0, 88.0, ALU.mult, ALU.min), "x" if st < 0 else None)
            own(v.tensor_scalar(NM[rows, :], M[rows, ::st], -1.0, None, ALU.mult))
            own(v.tensor_copy(C[rows, :], I[rows, ::st]), "rows" if st < 0 else None)
        dve.wait_ge(s["sel"], 2)
        dve.wait_ge(s["e"], 2)
        own(v.tensor_copy(CC[:], ps[:, 4, 0:256]), "x")

        def weigh(h, d):
            if d == 0:
                dve.wait_ge(s["ev"], 28 + 4 * h)
            dve.wait_ge(s["exp"], 7 * (2 * h + d) + 7)
            for i in range(TT):
                a, z, t0, t1 = span(d, i)
                w = E[:, h % 2, d, a:z]
                own(v.tensor_tensor(w, w, QK[:, i, t0:t1], ALU.mult), "m", wait=i == 3)

        def scale(h, d):
            dve.wait_ge(s["den"], 2 * h + d + 1)
            own(v.tensor_scalar(RC[:], ps[:, 6, :], -1.0, None, ALU.mult))
            own(v.tensor_tensor(RC[:], RC[:], ps[:, 6, :], ALU.max))
            own(v.tensor_tensor(RC[:], RC[:], ps[:, 7, :], ALU.max))
            own(v.reciprocal(RC[:], RC[:]))
            for i in range(TT):
                a, z, t0, t1 = span(d, i)
                w = E[:, h % 2, d, a:z]
                own(v.tensor_tensor(w, w, RC[:, t0:t1], ALU.mult), "sc" if i == 3 and d == 0 else None, wait=i >= 2)
            if d:
                for i in range(TT):
                    f, z = FCOL[i], BCOL[i] + i * P
                    own(v.tensor_tensor(E[:, h % 2, 0, f:f + P], E[:, h % 2, 0, f:f + P], E[:, h % 2, 1, z:z + P], ALU.add),
                        "sc" if i == 3 else None, wait=i >= 2)

        weigh(0, 0)
        weigh(0, 1)
        for h in range(NH):
            scale(h, 0)
            scale(h, 1)
            if h + 1 < NH:
                weigh(h + 1, 0)
                weigh(h + 1, 1)
        dve.wait_ge(s["sel"], 3)
        own(v.tensor_scalar(MU, ps[:, 6, 0:16], 1.0 / DV, None, ALU.mult))
        own(v.tensor_scalar(VAR, ps[:, 6, 16:32], 1.0 / DV, LN_EPS, ALU.mult, ALU.add))
        own(v.tensor_tensor(TMPA, MU, MU, ALU.mult))
        own(v.tensor_tensor(VAR, VAR, TMPA, ALU.subtract))
        rsqrt(own, VAR, RS, TMPA)
        own(v.scalar_tensor_tensor(NB, MU, -1.0, RS, ALU.mult, ALU.mult))

        def dg(h):
            for q, col in enumerate((RS, NB)):
                own(v.tensor_tensor(DG[:, h % 2, q, :].rearrange("p (j n) -> p j n", n=P), ident[:, None, :].to_broadcast([P, TT, P]),
                                    col[:, 4 * h:4 * h + 4][:, :, None].to_broadcast([P, TT, P]), ALU.mult), "dg")

        def gated(k):
            h = k // 2
            if k % 2 == 0:
                if h >= 2:
                    dve.wait_ge(s["bc"], h - 1)
                dg(h)
                dve.wait_ge(s["bc"], h + 1)
            y = YT[:, k % 2, :]
            own(v.tensor_tensor(y, H[:, k, :], ps[:, 2 * (h % 2), :], ALU.mult))
            own(v.tensor_tensor(y, y, ps[:, 2 * (h % 2) + 1, :], ALU.add))
            own(v.scalar_tensor_tensor(y, SIG[:, k, :], 1.0, y, ALU.add, ALU.mult), "y")

        gated(0)
        for k in range(KD):
            if k + 1 < KD:
                gated(k + 1)
            dve.wait_ge(s["e"], k + 3)
            own(v.scalar_tensor_tensor(XL[:, k, :], YT[:, k % 2, :], gain[:, k:k + 1], XH[:, k, :].bitcast(F32),
                                       ALU.mult, ALU.subtract), "x_ready")
        outproj_dve(b, e, e["n0"] + 13, residual)

    return dict(pe=pe, act=act, dve=dve)


MIXERS = dict(ev_attn=ev_attn, ev_mamba=ev_mamba, od=od_mixer, win=window_mixer, mlstm=mlstm_mixer)


CONSTS = dict(perm64=(0, P), perm32=(P, P), chunk=(2 * P, P), tri=(3 * P, P), tri_rev=(4 * P, P), le=(5 * P, P), gt=(6 * P, P),
              window=(7 * P, 3 * P), freq=(10 * P, 2), slope=(10 * P + 2, 16), half=(10 * P + 18, P),
              par=(11 * P + 18, 4))


def constants():
    import numpy as np
    c = np.zeros((P, 11 * P + 22), np.float32)
    r = np.arange(P)[:, None]
    m = np.arange(P)[None, :]

    def put(name, a):
        c[:, CONSTS[name][0]:CONSTS[name][0] + CONSTS[name][1]] = a

    put("perm64", np.where((m % 64 < 32) & (r == m + 32), -1.0, 0.0) + np.where((m % 64 >= 32) & (r == m - 32), 1.0, 0.0))
    put("perm32", np.where((m >= 64) & (m < 80) & (r == m + 16), -1.0, 0.0) + np.where((m >= 80) & (m < 96) & (r == m - 16), 1.0, 0.0))
    put("chunk", np.where(m // 64 > r // 64, -1e30, 0.0))
    put("tri", np.where(r > m, -1e30, 0.0))
    put("tri_rev", np.where(r < m, -1e30, 0.0))
    put("le", (r <= m) * 1.0)
    put("gt", (r > m) * 1.0)
    w = np.arange(3 * P)[None, :]
    rel = np.abs(r - w + P)
    put("window", np.where(rel <= P, rel, 1e30))
    f = np.zeros((P, 2))
    f[:, 0] = np.float64(10000.0) ** (-(np.arange(P) % 32) * (2.0 / 64))
    f[64:96, 1] = np.float64(10000.0) ** (-(np.arange(32) % 16) * (2.0 / 32))
    put("freq", f)
    put("slope", np.tile(-np.exp2(-8.0 * np.arange(1, 17) / 16) / 64 ** -0.5, (P, 1)))
    put("par", np.concatenate([r < 64, r >= 64, r // 16 % 2 == 0, r // 16 % 2 == 1], axis=1))
    put("half", np.where(m // 64 == r, 1.0, 0.0))
    return c


def full_plan(io):
    k8 = lambda w: w.rearrange("(kt p) n -> p kt n", p=P)
    RMS = dict(ln=False, keep=False)

    def ffn1(i, mean=False):
        return dict(kind="ffn", gate=(k8(io["ffn_gate"][i]), 0), up=(k8(io["ffn_up"][i]), 0), down=k8(io["ffn_down"][i]),
                    alpha=1.0, half=0.5, mean=mean)

    def ffn2(l, i):
        w = k8(io["ffn_w_in_2"][l, i])
        return dict(kind="ffn", gate=(w, 0), up=(w, FF), down=k8(io["ffn_w_out_2"][l, i]), alpha=ALPHA, half=0.25, mean=True)

    def ln(l, i):
        q = 3 * l + i
        return dict(kind="norm", ln=True, keep=True, gain=("ln_g", q), bias=("ln_b", q))

    return dict(
        load=dict(kind="load", mean=False), loadm=dict(kind="load", mean=True),
        n_mix0=dict(kind="norm", gain=("norm_mix", 0), **RMS), n_ffn0=dict(kind="norm", gain=("norm_ffn", 0), **RMS),
        n_mix1=dict(kind="norm", gain=("norm_mix", 1), **RMS), n_ffn1=dict(kind="norm", gain=("norm_ffn", 1), **RMS),
        n_final=dict(kind="norm", ln=False, keep=True, gain=("norm_final", 0)),
        ffn0=ffn1(0), ffn1=ffn1(1), f00=ffn2(0, 0), f01=ffn2(0, 1), f10=ffn2(1, 0), f11=ffn2(1, 1),
        ln00=ln(0, 0), ln01=ln(0, 1), ln02=ln(0, 2), ln10=ln(1, 0), ln11=ln(1, 1), ln12=ln(1, 2),
        store=dict(kind="store"),
        win=dict(kind="win", w_in=k8(io["at_w_in_2"][0]), w_out=k8(io["at_w_out_2"][0]), alpha=ALPHA),
        mlstm=dict(kind="mlstm", w_in=k8(io["ml_w_in_2"][0]), w_out=k8(io["ml_w_out_2"][0]), alpha=ALPHA),
        od=dict(kind="od", w_in=k8(io["od_w_in"][0]), w_out=k8(io["od_w_out"][0]), uq=k8(io["od_w_uq"][0]),
                ukv=k8(io["od_w_ukv"][0]), glu=k8(io["od_w_glu"][0]), alpha=1.0),
        ev_attn=dict(kind="ev_attn", w_in=k8(io["ev_w_in"][0]), w_out=k8(io["ev_w_out"][0]), alpha=1.0),
        ev_mamba=dict(kind="ev_mamba", w_in=k8(io["ev_w_in"][0]), w_out=k8(io["ev_w_out"][0]), alpha=1.0),
    )


_STAGES = "load n_mix0 ev_attn ev_mamba n_ffn0 ffn0 n_mix1 od n_ffn1 ffn1 n_final f00 ln00 mlstm ln01 f01 ln02 f10 ln10 win ln11 f11 ln12 store".split()
_INS = ['x', 'positions', 'norm_mix', 'ev_w_in', 'ev_conv_w', 'ev_conv_b', 'ev_dt_bias', 'ev_a_log', 'ev_d_skip',
        'ev_gate_norm', 'ev_lambdas', 'ev_subln', 'ev_w_out', 'od_w_in', 'od_lam_re', 'od_lam_im', 'od_log_step',
        'od_b_re', 'od_b_im', 'od_c_re', 'od_c_im', 'od_d_skip', 'od_w_glu', 'od_b_glu', 'od_q_norm', 'od_w_uq',
        'od_kv_norm', 'od_w_ukv', 'od_w_out', 'norm_ffn', 'ffn_gate', 'ffn_up', 'ffn_down', 'norm_final', 'ffn_w_in_2',
        'ffn_w_out_2', 'ln_g_2', 'ln_b_2', 'ml_w_in_2', 'ml_gate_b_2', 'ml_norm_g_2', 'ml_w_out_2', 'at_w_in_2',
        'at_sink_2', 'at_w_out_2']


def kernel(**inputs):
    import numpy as np
    import concourse.bacc as bacc
    from concourse.bass_utils import run_bass_kernel_spmd

    nc = bacc.Bacc("TRN2", target_bir_lowering=False, num_devices=1)
    arrays, io = {}, {}
    for name in _INS:
        a = np.ascontiguousarray(inputs[name])
        arrays[f"in_{name}"] = a
        io[name] = nc.dram_tensor(f"in_{name}", a.shape, mybir.dt.from_np(a.dtype), kind="ExternalInput").ap()
    arrays["constants"] = constants()
    io["constants"] = nc.dram_tensor("constants", arrays["constants"].shape, F32, kind="ExternalInput").ap()
    io["out"] = nc.dram_tensor("out_0", (1, T, D), F32, kind="ExternalOutput").ap()
    plans = full_plan(io)
    build(nc, io, [plans[s] for s in _STAGES])
    r = run_bass_kernel_spmd(nc, [arrays], core_ids=[0])
    return r.results[0]["out_0"]
```
